# Optimizing a Trainium2 kernel written in Bass

```python
import jax, jax.numpy as jnp
from jax import lax
import numpy as np

D_MODEL = 1024
BATCH = 1
SEQ = 512
DEPTH = 2

GRID_W = 64
CTX_LEN = 256
N_EVEN = (DEPTH + 1) // 2
N_ODD = DEPTH // 2

MLA_HEADS = 8
MLA_Q_RANK = 384
MLA_KV_RANK = 256
MLA_NOPE = 64
MLA_ROPE = 32
MLA_V = 64
MLA_QK = MLA_NOPE + MLA_ROPE
GQA_HEADS = 8
GQA_KV_HEADS = 2
GQA_DIM = 64
EVEN_SPLITS = (MLA_Q_RANK, MLA_KV_RANK, MLA_ROPE, GQA_HEADS * GQA_DIM,
               GQA_KV_HEADS * GQA_DIM, GQA_KV_HEADS * GQA_DIM)
EVEN_IN = sum(EVEN_SPLITS)
EVEN_MIX = MLA_HEADS * MLA_V + GQA_HEADS * GQA_DIM
MLSTM_HEADS = 8
MLSTM_QK = 64
MLSTM_V = 128
MLSTM_CONV = 3
MLSTM_CHUNK = 64
ODD_SPLITS = (2 * MLSTM_HEADS * MLSTM_QK, MLSTM_HEADS * MLSTM_V, MLSTM_HEADS * MLSTM_V, 4 * MLSTM_HEADS)
ODD_IN = sum(ODD_SPLITS)
D_FF = 2816
FFN_CONV = 3

Q_BLOCK = 128
ROPE_THETA = 10000.0
EPS = 1e-6


def rmsnorm(x, g):
    xf = x.astype(jnp.float32)
    y = xf * lax.rsqrt(jnp.mean(xf * xf, axis=-1, keepdims=True) + EPS)
    return (y * g.astype(jnp.float32)).astype(x.dtype)

def modulate(h, shift, scale):
    return h * (1 + scale) + shift

def split_cols(p, sizes):
    return jnp.split(p, np.cumsum(sizes)[:-1].tolist(), axis=-1)

def dwconv(x, w, b):
    width, T = w.shape[0], x.shape[1]
    left = (width - 1) // 2
    xp = jnp.pad(x, ((0, 0), (left, width - 1 - left), (0, 0)))
    return sum(xp[:, j:j + T] * w[j] for j in range(width)) + b

def axial_rope_tables(n_tokens, rot_dim):
    rows = n_tokens // GRID_W
    row = jnp.repeat(jnp.arange(rows), GRID_W).astype(jnp.float32)
    col = jnp.tile(jnp.arange(GRID_W), rows).astype(jnp.float32)
    n_freq = rot_dim // 4
    inv = ROPE_THETA ** (-jnp.arange(n_freq, dtype=jnp.float32) / n_freq)
    a_r, a_c = row[:, None] * inv, col[:, None] * inv
    ang = jnp.concatenate([a_r, a_r, a_c, a_c], axis=-1)
    return jnp.cos(ang), jnp.sin(ang)

def apply_rope(x, cos, sin):
    a1, a2, b1, b2 = jnp.split(x, 4, axis=-1)
    rot = jnp.concatenate([-a2, a1, -b2, b1], axis=-1)
    shape = (1, x.shape[1]) + (1,) * (x.ndim - 3) + (x.shape[-1],)
    return x * cos.reshape(shape).astype(x.dtype) + rot * sin.reshape(shape).astype(x.dtype)

def attend(q, k, v):
    B, T, G, R, dk = q.shape
    nb = T // Q_BLOCK
    scale = dk ** -0.5
    qb = jnp.moveaxis(q.reshape(B, nb, Q_BLOCK, G, R, dk), 1, 0)

    def block(qi):
        s = jnp.einsum('bqgrd,bsgd->bgrqs', qi, k).astype(jnp.float32) * scale
        p = jax.nn.softmax(s, axis=-1).astype(v.dtype)
        return jnp.einsum('bgrqs,bsgd->bqgrd', p, v)

    out = lax.map(block, qb)
    return jnp.moveaxis(out, 0, 1).reshape(B, T, G, R, v.shape[-1])

def mla_q(cq, g_qa, w_qb, g_q, rope):
    B, T, _ = cq.shape
    q = jnp.dot(rmsnorm(cq, g_qa), w_qb).reshape(B, T, MLA_HEADS, MLA_QK)
    q = rmsnorm(q, g_q)
    if rope is not None:
        q = jnp.concatenate([q[..., :MLA_NOPE], apply_rope(q[..., MLA_NOPE:], *rope)], axis=-1)
    return q[:, :, :, None, :]

def mla_kv(ckv, k_rope, g_kva, w_kvb, g_k, rope):
    B, T, _ = ckv.shape
    kv = jnp.dot(rmsnorm(ckv, g_kva), w_kvb).reshape(B, T, MLA_HEADS, MLA_NOPE + MLA_V)
    k_nope, v = kv[..., :MLA_NOPE], kv[..., MLA_NOPE:]
    k_pe = jnp.broadcast_to(k_rope[:, :, None, :], (B, T, MLA_HEADS, MLA_ROPE))
    k = rmsnorm(jnp.concatenate([k_nope, k_pe], axis=-1), g_k)
    if rope is not None:
        k = jnp.concatenate([k[..., :MLA_NOPE], apply_rope(k[..., MLA_NOPE:], *rope)], axis=-1)
    return k, v

def gqa_q(q, g_q, rope):
    B, T, _ = q.shape
    q = rmsnorm(q.reshape(B, T, GQA_HEADS, GQA_DIM), g_q)
    if rope is not None:
        q = apply_rope(q, *rope)
    return q.reshape(B, T, GQA_KV_HEADS, GQA_HEADS // GQA_KV_HEADS, GQA_DIM)

def gqa_kv(k, v, g_k, rope):
    B, T, _ = k.shape
    k = rmsnorm(k.reshape(B, T, GQA_KV_HEADS, GQA_DIM), g_k)
    if rope is not None:
        k = apply_rope(k, *rope)
    return k, v.reshape(B, T, GQA_KV_HEADS, GQA_DIM)

def even_mixer(h_lat, h_ctx, w_in, g_qa, w_qb, g_kva, w_kvb, g_mq, g_mk, g_gq, g_gk, w_out,
               rope_mla, rope_gqa, need_ctx_out):
    cq_l, ckv_l, kr_l, gq_l, gk_l, gv_l = split_cols(jnp.dot(h_lat, w_in), EVEN_SPLITS)
    cq_c, ckv_c, kr_c, gq_c, gk_c, gv_c = split_cols(jnp.dot(h_ctx, w_in), EVEN_SPLITS)
    ka_c, va_c = mla_kv(ckv_c, kr_c, g_kva, w_kvb, g_mk, None)
    ka_l, va_l = mla_kv(ckv_l, kr_l, g_kva, w_kvb, g_mk, rope_mla)
    kb_c, vb_c = gqa_kv(gk_c, gv_c, g_gk, None)
    kb_l, vb_l = gqa_kv(gk_l, gv_l, g_gk, rope_gqa)
    ka, va = jnp.concatenate([ka_c, ka_l], axis=1), jnp.concatenate([va_c, va_l], axis=1)
    kb, vb = jnp.concatenate([kb_c, kb_l], axis=1), jnp.concatenate([vb_c, vb_l], axis=1)

    def merge(o_a, o_b):
        B, T = o_a.shape[:2]
        return jnp.dot(jnp.concatenate([o_a.reshape(B, T, -1), o_b.reshape(B, T, -1)], axis=-1), w_out)

    out_lat = merge(attend(mla_q(cq_l, g_qa, w_qb, g_mq, rope_mla), ka, va),
                    attend(gqa_q(gq_l, g_gq, rope_gqa), kb, vb))
    out_ctx = None
    if need_ctx_out:
        out_ctx = merge(attend(mla_q(cq_c, g_qa, w_qb, g_mq, None), ka_c, va_c),
                        attend(gqa_q(gq_c, g_gq, None), kb_c, vb_c))
    return out_lat, out_ctx

def mlstm_inputs(h, w_in, conv_w, conv_b, gate_b):
    B, T, _ = h.shape
    qk, v, o, g = split_cols(jnp.dot(h, w_in), ODD_SPLITS)
    q, k = jnp.split(jax.nn.silu(dwconv(qk, conv_w, conv_b)), 2, axis=-1)

    def heads(t, d):
        return jnp.swapaxes(t.reshape(B, T, MLSTM_HEADS, d), 1, 2).astype(jnp.float32)

    g = (g + gate_b).astype(jnp.float32).reshape(B, T, 4, MLSTM_HEADS)
    g = jnp.transpose(g, (2, 0, 3, 1))
    gates = (g[0], jax.nn.log_sigmoid(g[1]), g[2], jax.nn.log_sigmoid(g[3]))
    return heads(q, MLSTM_QK), heads(k, MLSTM_QK) * MLSTM_QK ** -0.5, heads(v, MLSTM_V), o, gates

def mlstm_state_update(state, k, v, log_i, b):
    C, n, m = state
    b_last = b[..., -1]
    a = b_last[..., None] - b + log_i
    m_new = jnp.maximum(b_last + m, jnp.max(a, axis=-1))
    decay = jnp.exp(b_last + m - m_new)
    w = jnp.exp(a - m_new[..., None])
    C_new = decay[..., None, None] * C + jnp.einsum('bhs,bhsv,bhsd->bhvd', w, v, k)
    n_new = decay[..., None] * n + jnp.einsum('bhs,bhsd->bhd', w, k)
    return (C_new, n_new, m_new)

def mlstm_chunkwise(q, k, v, log_i, log_f, state0):
    B, H, T, dk = q.shape
    dv = v.shape[-1]
    L = MLSTM_CHUNK
    nc = T // L
    lower = jnp.tril(jnp.ones((L, L), dtype=bool))

    def chunks(t):
        return jnp.moveaxis(t.reshape((B, H, nc, L) + t.shape[3:]), 2, 0)

    def step(state, inp):
        C, n, m = state
        qc, kc, vc, ic, fc = inp
        b = jnp.cumsum(fc, axis=-1)
        logw = jnp.where(lower, b[..., :, None] - b[..., None, :] + ic[..., None, :], -jnp.inf)
        log_inter = b + m[..., None]
        m_t = jnp.maximum(log_inter, jnp.max(logw, axis=-1))
        w_inter = jnp.exp(log_inter - m_t)
        s = jnp.einsum('bhtd,bhsd->bhts', qc, kc) * jnp.exp(logw - m_t[..., None])
        num = w_inter[..., None] * jnp.einsum('bhvd,bhtd->bhtv', C, qc) + jnp.einsum('bhts,bhsv->bhtv', s, vc)
        den = w_inter * jnp.einsum('bhd,bhtd->bht', n, qc) + jnp.sum(s, axis=-1)
        h = num / jnp.maximum(jnp.abs(den), jnp.exp(-m_t))[..., None]
        return mlstm_state_update(state, kc, vc, ic, b), h

    state, h = lax.scan(step, state0, (chunks(q), chunks(k), chunks(v), chunks(log_i), chunks(log_f)))
    return jnp.moveaxis(h, 0, 2).reshape(B, H, T, dv), state

def mlstm_direction(q_l, k_l, v_l, li_l, lf_l, q_c, k_c, v_c, li_c, lf_c, need_ctx_out):
    B, H = q_l.shape[:2]
    state0 = (jnp.zeros((B, H, MLSTM_V, MLSTM_QK), jnp.float32),
              jnp.zeros((B, H, MLSTM_QK), jnp.float32),
              jnp.zeros((B, H), jnp.float32))
    if need_ctx_out:
        h_c, state_c = mlstm_chunkwise(q_c, k_c, v_c, li_c, lf_c, state0)
    else:
        h_c = None
        state_c = mlstm_state_update(state0, k_c, v_c, li_c, jnp.cumsum(lf_c, axis=-1))
    h_l, _ = mlstm_chunkwise(q_l, k_l, v_l, li_l, lf_l, state_c)
    return h_l, h_c

def odd_mixer(h_lat, h_ctx, w_in, conv_w, conv_b, gate_b, out_g, w_out, need_ctx_out):
    q_l, k_l, v_l, o_l, g_l = mlstm_inputs(h_lat, w_in, conv_w, conv_b, gate_b)
    q_c, k_c, v_c, o_c, g_c = mlstm_inputs(h_ctx, w_in, conv_w, conv_b, gate_b)

    def rev(t):
        return jnp.flip(t, axis=2)

    hf_l, hf_c = mlstm_direction(q_l, k_l, v_l, g_l[0], g_l[1], q_c, k_c, v_c, g_c[0], g_c[1], need_ctx_out)
    hb_l, hb_c = mlstm_direction(rev(q_l), rev(k_l), rev(v_l), rev(g_l[2]), rev(g_l[3]),
                                 rev(q_c), rev(k_c), rev(v_c), rev(g_c[2]), rev(g_c[3]), need_ctx_out)

    def readout(hf, hb, o):
        h = jnp.swapaxes(hf + rev(hb), 1, 2)
        B, T = h.shape[:2]
        h = rmsnorm(h, out_g).reshape(B, T, -1).astype(o.dtype)
        return jnp.dot(h * jax.nn.sigmoid(o), w_out)

    out_lat = readout(hf_l, hb_l, o_l)
    out_ctx = readout(hf_c, hb_c, o_c) if need_ctx_out else None
    return out_lat, out_ctx

def conv_ffn(h, w_up, conv_w, conv_b, w_down):
    gate, val = jnp.split(jnp.dot(h, w_up), 2, axis=-1)
    return jnp.dot(jax.nn.silu(dwconv(gate, conv_w, conv_b)) * val, w_down)

def first_inputs(seed: int = 0) -> dict:
    key = jax.random.key(seed)
    keys = jax.random.split(key, 40)
    counter = iter(range(40))
    D = D_MODEL

    def nrm(shape, scale):
        return jax.random.normal(keys[next(counter)], shape, jnp.float32) * scale

    def gain(shape):
        return 1.0 + nrm(shape, 0.05)

    H = MLSTM_HEADS
    i_bias = nrm((N_ODD, 2, 1, H), 0.1)
    f_bias = jnp.linspace(3.0, 6.0, H, dtype=jnp.float32) + nrm((N_ODD, 2, 1, H), 0.1)
    ml_gate_b = jnp.concatenate([i_bias, f_bias], axis=2).reshape(N_ODD, 4 * H)
    return {
        'x': nrm((BATCH, SEQ, D), 1.0),
        'c': nrm((BATCH, D), 1.0),
        'ctx': nrm((BATCH, CTX_LEN, D), 1.0),
        'c_ctx': nrm((D,), 1.0),
        'ada_w': nrm((DEPTH, D, 6 * D), 0.5 * D ** -0.5),
        'ada_b': nrm((DEPTH, 6 * D), 0.02),
        'norm1_g': gain((DEPTH, D)),
        'norm2_g': gain((DEPTH, D)),
        'ffn_w_up': nrm((DEPTH, D, 2 * D_FF), D ** -0.5),
        'ffn_conv_w': nrm((DEPTH, FFN_CONV, D_FF), 0.5),
        'ffn_conv_b': nrm((DEPTH, D_FF), 0.02),
        'ffn_w_down': nrm((DEPTH, D_FF, D), D_FF ** -0.5),
        'att_w_in': nrm((N_EVEN, D, EVEN_IN), D ** -0.5),
        'mla_qa_g': gain((N_EVEN, MLA_Q_RANK)),
        'mla_w_qb': nrm((N_EVEN, MLA_Q_RANK, MLA_HEADS * MLA_QK), MLA_Q_RANK ** -0.5),
        'mla_kva_g': gain((N_EVEN, MLA_KV_RANK)),
        'mla_w_kvb': nrm((N_EVEN, MLA_KV_RANK, MLA_HEADS * (MLA_NOPE + MLA_V)), MLA_KV_RANK ** -0.5),
        'mla_q_g': gain((N_EVEN, MLA_QK)),
        'mla_k_g': gain((N_EVEN, MLA_QK)),
        'gqa_q_g': gain((N_EVEN, GQA_DIM)),
        'gqa_k_g': gain((N_EVEN, GQA_DIM)),
        'att_w_out': nrm((N_EVEN, EVEN_MIX, D), EVEN_MIX ** -0.5),
        'ml_w_in': nrm((N_ODD, D, ODD_IN), D ** -0.5),
        'ml_conv_w': nrm((N_ODD, MLSTM_CONV, 2 * H * MLSTM_QK), 0.5),
        'ml_conv_b': nrm((N_ODD, 2 * H * MLSTM_QK), 0.02),
        'ml_gate_b': ml_gate_b,
        'ml_out_g': gain((N_ODD, H, MLSTM_V)),
        'ml_w_out': nrm((N_ODD, H * MLSTM_V, D), (H * MLSTM_V) ** -0.5),
    }

def first_block(x, c, ctx, c_ctx, ada_w, ada_b, norm1_g, norm2_g, ffn_w_up, ffn_conv_w, ffn_conv_b,
              ffn_w_down, att_w_in, mla_qa_g, mla_w_qb, mla_kva_g, mla_w_kvb, mla_q_g, mla_k_g,
              gqa_q_g, gqa_k_g, att_w_out, ml_w_in, ml_conv_w, ml_conv_b, ml_gate_b, ml_out_g, ml_w_out):
    n_lat = x.shape[1]
    rope_mla = axial_rope_tables(n_lat, MLA_ROPE)
    rope_gqa = axial_rope_tables(n_lat, GQA_DIM)
    for layer in range(DEPTH):
        need_ctx_out = layer < DEPTH - 1
        j = layer // 2
        mod_lat = (jnp.dot(jax.nn.silu(c), ada_w[layer]) + ada_b[layer])[:, None, :]
        mod_ctx = jnp.dot(jax.nn.silu(c_ctx), ada_w[layer]) + ada_b[layer]
        sh1, sc1, gt1, sh2, sc2, gt2 = jnp.split(mod_lat, 6, axis=-1)
        csh1, csc1, cgt1, csh2, csc2, cgt2 = jnp.split(mod_ctx, 6, axis=-1)
        h_lat = modulate(rmsnorm(x, norm1_g[layer]), sh1, sc1)
        h_ctx = modulate(rmsnorm(ctx, norm1_g[layer]), csh1, csc1)
        if layer % 2 == 0:
            out_lat, out_ctx = even_mixer(h_lat, h_ctx, att_w_in[j], mla_qa_g[j], mla_w_qb[j], mla_kva_g[j],
                                          mla_w_kvb[j], mla_q_g[j], mla_k_g[j], gqa_q_g[j], gqa_k_g[j],
                                          att_w_out[j], rope_mla, rope_gqa, need_ctx_out)
        else:
            out_lat, out_ctx = odd_mixer(h_lat, h_ctx, ml_w_in[j], ml_conv_w[j], ml_conv_b[j], ml_gate_b[j],
                                         ml_out_g[j], ml_w_out[j], need_ctx_out)
        x = x + gt1 * out_lat
        x = x + gt2 * conv_ffn(modulate(rmsnorm(x, norm2_g[layer]), sh2, sc2),
                               ffn_w_up[layer], ffn_conv_w[layer], ffn_conv_b[layer], ffn_w_down[layer])
        if need_ctx_out:
            ctx = ctx + cgt1 * out_ctx
            ctx = ctx + cgt2 * conv_ffn(modulate(rmsnorm(ctx, norm2_g[layer]), csh2, csc2),
                                       ffn_w_up[layer], ffn_conv_w[layer], ffn_conv_b[layer], ffn_w_down[layer])
    return x


HEAD_DIM = 64
ATTN_HEADS = 8
KV_HEADS = 2
Q_PER_KV = ATTN_HEADS // KV_HEADS
ATTN_WIDTH = ATTN_HEADS * HEAD_DIM
KV_WIDTH = KV_HEADS * HEAD_DIM
WINDOW = 128
BLOCK = 128
FOURIER_GROUPS = 4
FOURIER_GROUP_DIM = 64
FOURIER_WIDTH = FOURIER_GROUPS * FOURIER_GROUP_DIM
CONV_GROUPS = 4
CONV_WIDTH = 256
CONV_TAPS = 3
MIX_WIDTH = ATTN_WIDTH + FOURIER_WIDTH + CONV_WIDTH
PROJ_SIZES = (ATTN_WIDTH, KV_WIDTH, KV_WIDTH, ATTN_WIDTH,
              FOURIER_WIDTH, FOURIER_WIDTH,
              CONV_WIDTH, CONV_WIDTH, CONV_WIDTH, CONV_WIDTH)
PROJ_WIDTH = 2 * ATTN_WIDTH + 2 * KV_WIDTH + 2 * FOURIER_WIDTH + 4 * CONV_WIDTH
ROPE_FREQS = HEAD_DIM // 4
ROPE_BASE = 10000.0
NORM_EPS = 1e-6


def rmsnorm_2(x, g):
    xf = x.astype(jnp.float32)
    y = xf * lax.rsqrt(jnp.mean(xf * xf, axis=-1, keepdims=True) + NORM_EPS)
    return (y * g.astype(jnp.float32)).astype(x.dtype)

def split_cols_2(p, sizes):
    out = []
    start = 0
    for s in sizes:
        out.append(p[..., start:start + s])
        start += s
    return out

def axial_rope_tables_2(n):
    rows = n // GRID_W
    row = jnp.repeat(jnp.arange(rows, dtype=jnp.float32), GRID_W)
    col = jnp.tile(jnp.arange(GRID_W, dtype=jnp.float32), rows)
    inv_freq = jnp.power(ROPE_BASE, -jnp.arange(ROPE_FREQS, dtype=jnp.float32) / ROPE_FREQS)
    ang = jnp.concatenate([row[:, None] * inv_freq, col[:, None] * inv_freq], axis=-1)
    return jnp.cos(ang), jnp.sin(ang)

def apply_axial_rope(x, cos, sin):
    b, n, h, d = x.shape
    xr = x.astype(jnp.float32).reshape(b, n, h, 2, 2, ROPE_FREQS)
    x1 = xr[..., 0, :]
    x2 = xr[..., 1, :]
    cs = cos.reshape(n, 1, 2, ROPE_FREQS)
    sn = sin.reshape(n, 1, 2, ROPE_FREQS)
    out = jnp.stack([x1 * cs - x2 * sn, x1 * sn + x2 * cs], axis=-2)
    return out.reshape(b, n, h, d).astype(x.dtype)

def sink_softmax(s, sink_b):
    m = jnp.maximum(jnp.max(s, axis=-1, keepdims=True), sink_b)
    e = jnp.exp(s - m)
    return e / (jnp.sum(e, axis=-1, keepdims=True) + jnp.exp(sink_b - m))

def window_attention(q, k, v, kc, vc, sink_b):
    b, n = q.shape[:2]
    nb = n // BLOCK
    span = BLOCK + 2 * WINDOW
    nc = kc.shape[1]
    qb = (q * (HEAD_DIM ** -0.5)).reshape(b, nb, BLOCK, KV_HEADS, Q_PER_KV, HEAD_DIM).transpose(1, 0, 2, 3, 4, 5)
    pad = ((0, 0), (WINDOW, WINDOW), (0, 0), (0, 0))
    kp = jnp.pad(k, pad)
    vp = jnp.pad(v, pad)
    offs_q = jnp.arange(BLOCK)
    offs_k = jnp.arange(span) - WINDOW

    def one_block(args):
        qi, i = args
        start = i * BLOCK
        ks = lax.dynamic_slice_in_dim(kp, start, span, axis=1)
        vs = lax.dynamic_slice_in_dim(vp, start, span, axis=1)
        qpos = start + offs_q
        kpos = start + offs_k
        valid = (jnp.abs(qpos[:, None] - kpos[None, :]) <= WINDOW) & (kpos >= 0)[None, :] & (kpos < n)[None, :]
        s_loc = jnp.einsum('bqkgd,bnkd->bkgqn', qi, ks).astype(jnp.float32)
        s_loc = jnp.where(valid, s_loc, -jnp.inf)
        s_ctx = jnp.einsum('bqkgd,bnkd->bkgqn', qi, kc).astype(jnp.float32)
        p = sink_softmax(jnp.concatenate([s_ctx, s_loc], axis=-1), sink_b).astype(v.dtype)
        return (jnp.einsum('bkgqn,bnkd->bqkgd', p[..., :nc], vc)
                + jnp.einsum('bkgqn,bnkd->bqkgd', p[..., nc:], vs))

    o = lax.map(one_block, (qb, jnp.arange(nb)))
    return o.transpose(1, 0, 2, 3, 4, 5).reshape(b, n, ATTN_WIDTH)

def context_attention(q, k, v, sink_b):
    b, n = q.shape[:2]
    qg = (q * (HEAD_DIM ** -0.5)).reshape(b, n, KV_HEADS, Q_PER_KV, HEAD_DIM)
    s = jnp.einsum('bqkgd,bnkd->bkgqn', qg, k).astype(jnp.float32)
    p = sink_softmax(s, sink_b).astype(v.dtype)
    return jnp.einsum('bkgqn,bnkd->bqkgd', p, v).reshape(b, n, ATTN_WIDTH)

def fourier_mix(u, w_f):
    b, n, _ = u.shape
    ug = u.reshape(b, n, FOURIER_GROUPS, FOURIER_GROUP_DIM).astype(jnp.float32)
    f = jnp.fft.fft2(ug, axes=(1, 3), norm='ortho').real.astype(u.dtype)
    return jnp.einsum('bngc,gcd->bngd', f, w_f).reshape(b, n, FOURIER_WIDTH)

def short_conv_mix(z, b_gate, c_gate, w, bias):
    t = c_gate * z
    tp = jnp.pad(t, ((0, 0), (1, 1), (0, 0)))
    y = tp[:, :-2] * w[0] + tp[:, 1:-1] * w[1] + tp[:, 2:] * w[2] + bias
    return b_gate * y

def gated_merge(a, ga, f, gf, s, gc, w_out):
    h = jnp.concatenate([a * jax.nn.silu(ga), f * jax.nn.silu(gf), s * jax.nn.silu(gc)], axis=-1)
    return h @ w_out

def layer(x, ctx, c, c_ctx, w_mod, b_mod, g_pre, g_post, w_in, w_out, sink, w_fourier, conv_w, conv_b,
          cos, sin, update_ctx):
    b, n = x.shape[:2]
    nc = ctx.shape[1]
    shift, scale, gate = jnp.split(jax.nn.silu(c) @ w_mod + b_mod, 3, axis=-1)
    shift_c, scale_c, gate_c = jnp.split(jax.nn.silu(c_ctx) @ w_mod + b_mod, 3, axis=-1)
    sink_b = sink.astype(jnp.float32).reshape(1, KV_HEADS, Q_PER_KV, 1, 1)

    hx = rmsnorm_2(x, g_pre) * (1 + scale[:, None]) + shift[:, None]
    hc = rmsnorm_2(ctx, g_pre) * (1 + scale_c) + shift_c

    if update_ctx:
        qc, kc, vc, gac, ufc, gfc, zcc, bcc, ccc, gcc = split_cols_2(hc @ w_in, PROJ_SIZES)
    else:
        kc, vc = split_cols_2(hc @ w_in[:, ATTN_WIDTH:ATTN_WIDTH + 2 * KV_WIDTH], (KV_WIDTH, KV_WIDTH))
    kc = kc.reshape(b, nc, KV_HEADS, HEAD_DIM)
    vc = vc.reshape(b, nc, KV_HEADS, HEAD_DIM)

    q, k, v, ga, uf, gf, zc, bc, cc, gc = split_cols_2(hx @ w_in, PROJ_SIZES)
    q = apply_axial_rope(q.reshape(b, n, ATTN_HEADS, HEAD_DIM), cos, sin)
    k = apply_axial_rope(k.reshape(b, n, KV_HEADS, HEAD_DIM), cos, sin)
    v = v.reshape(b, n, KV_HEADS, HEAD_DIM)
    a = window_attention(q, k, v, kc, vc, sink_b)
    f = fourier_mix(uf, w_fourier)
    s = short_conv_mix(zc, bc, cc, conv_w, conv_b)
    y = gated_merge(a, ga, f, gf, s, gc, w_out)
    x_new = x + gate[:, None] * rmsnorm_2(y, g_post)

    if update_ctx:
        ac = context_attention(qc.reshape(b, nc, ATTN_HEADS, HEAD_DIM), kc, vc, sink_b)
        fc = fourier_mix(ufc, w_fourier)
        sc = short_conv_mix(zcc, bcc, ccc, conv_w, conv_b)
        yc = gated_merge(ac, gac, fc, gfc, sc, gcc, w_out)
        ctx = ctx + gate_c * rmsnorm_2(yc, g_post)
    return x_new, ctx

def second_inputs(seed: int = 0) -> dict:
    key = jax.random.key(seed)
    ks = jax.random.split(key, 14)
    nrm = jax.random.normal
    x = nrm(ks[0], (BATCH, SEQ, D_MODEL), jnp.float32)
    c = nrm(ks[1], (BATCH, D_MODEL), jnp.float32)
    ctx = nrm(ks[2], (BATCH, CTX_LEN, D_MODEL), jnp.float32)
    c_ctx = nrm(ks[3], (D_MODEL,), jnp.float32)
    w_mod = nrm(ks[4], (DEPTH, D_MODEL, 3 * D_MODEL), jnp.float32) * (0.5 * D_MODEL ** -0.5)
    b_mod = 0.01 * nrm(ks[5], (DEPTH, 3 * D_MODEL), jnp.float32)
    g_pre = 1.0 + 0.05 * nrm(ks[6], (DEPTH, D_MODEL), jnp.float32)
    g_post = 1.0 + 0.05 * nrm(ks[7], (DEPTH, D_MODEL), jnp.float32)
    w_in = nrm(ks[8], (DEPTH, D_MODEL, PROJ_WIDTH), jnp.float32) * (D_MODEL ** -0.5)
    w_out = nrm(ks[9], (DEPTH, MIX_WIDTH, D_MODEL), jnp.float32) * (MIX_WIDTH ** -0.5)
    sink = 0.5 * nrm(ks[10], (DEPTH, ATTN_HEADS), jnp.float32)
    w_fourier = nrm(ks[11], (DEPTH, FOURIER_GROUPS, FOURIER_GROUP_DIM, FOURIER_GROUP_DIM), jnp.float32) * (FOURIER_GROUP_DIM ** -0.5)
    conv_w = nrm(ks[12], (DEPTH, CONV_TAPS, CONV_WIDTH), jnp.float32) * (CONV_TAPS ** -0.5)
    conv_b = 0.01 * nrm(ks[13], (DEPTH, CONV_WIDTH), jnp.float32)
    return {'x': x, 'c': c, 'ctx': ctx, 'c_ctx': c_ctx, 'w_mod': w_mod, 'b_mod': b_mod,
            'g_pre': g_pre, 'g_post': g_post, 'w_in': w_in, 'w_out': w_out, 'sink': sink,
            'w_fourier': w_fourier, 'conv_w': conv_w, 'conv_b': conv_b}

def second_block(x, c, ctx, c_ctx, w_mod, b_mod, g_pre, g_post, w_in, w_out, sink, w_fourier, conv_w, conv_b):
    cos, sin = axial_rope_tables_2(x.shape[1])
    for l in range(DEPTH):
        x, ctx = layer(x, ctx, c, c_ctx, w_mod[l], b_mod[l], g_pre[l], g_post[l], w_in[l], w_out[l],
                       sink[l], w_fourier[l], conv_w[l], conv_b[l], cos, sin, l < DEPTH - 1)
    return x


def setup_inputs(seed=0):
    out = dict(first_inputs(seed))
    for name, value in second_inputs(seed + 1).items():
        if name != "x":
            out[name + "_2"] = value
    return out


def reference(
    x, c, ctx, c_ctx, ada_w, ada_b, norm1_g, norm2_g, ffn_w_up, ffn_conv_w, ffn_conv_b,
    ffn_w_down, att_w_in, mla_qa_g, mla_w_qb, mla_kva_g, mla_w_kvb, mla_q_g, mla_k_g, gqa_q_g,
    gqa_k_g, att_w_out, ml_w_in, ml_conv_w, ml_conv_b, ml_gate_b, ml_out_g, ml_w_out, c_2,
    ctx_2, c_ctx_2, w_mod_2, b_mod_2, g_pre_2, g_post_2, w_in_2, w_out_2, sink_2, w_fourier_2,
    conv_w_2, conv_b_2,
):
    x = first_block(
        x, c, ctx, c_ctx, ada_w, ada_b, norm1_g, norm2_g, ffn_w_up, ffn_conv_w, ffn_conv_b,
        ffn_w_down, att_w_in, mla_qa_g, mla_w_qb, mla_kva_g, mla_w_kvb, mla_q_g, mla_k_g,
        gqa_q_g, gqa_k_g, att_w_out, ml_w_in, ml_conv_w, ml_conv_b, ml_gate_b, ml_out_g,
        ml_w_out,
    )
    return second_block(
        x, c_2, ctx_2, c_ctx_2, w_mod_2, b_mod_2, g_pre_2, g_post_2, w_in_2, w_out_2, sink_2,
        w_fourier_2, conv_w_2, conv_b_2,
    )


_drawn_inputs = setup_inputs


def setup_inputs(seed=0):
    import zlib

    import numpy as np

    out = dict(_drawn_inputs(seed))
    spreads = {}
    factors = {'norm1_g': 4.199,
     'norm2_g': 2.668,
     'ffn_conv_b': 8.0,
     'mla_qa_g': 8.0,
     'mla_w_qb': 2.957,
     'mla_kva_g': 8.0,
     'mla_q_g': 8.0,
     'mla_k_g': 8.0,
     'gqa_q_g': 8.0,
     'gqa_k_g': 8.0,
     'ml_conv_b': 40.434,
     'ml_out_g': 6.998,
     'b_mod_2': 3.332,
     'g_post_2': 8.046,
     'sink_2': 24.367,
     'conv_b_2': 8.0}
    for name, (base, spread) in spreads.items():
        noise = np.random.default_rng([zlib.crc32(name.encode()), seed]).standard_normal(out[name].shape)
        drawn = base * np.exp(spread * noise) if base else spread * noise
        out[name] = __import__('jax').numpy.asarray(drawn.astype(out[name].dtype))
    for name, factor in factors.items():
        out[name] = (out[name] * factor).astype(out[name].dtype)
    return out
```

```python
from contextlib import ExitStack

import numpy as np

import concourse.bass as bass
from concourse import mybir

F32 = mybir.dt.float32
F32R = mybir.dt.float32r
ALU = mybir.AluOpType
AF = mybir.ActivationFunctionType
AX = mybir.AxisListType.X

P = 128
D = 1024
KD = D // P
CTX, LAT = 256, 512
TOK = CTX + LAT
HEADS = 8
FF = 2816
FT = FF // P
GROUPS = [(0, 6), (6, 12), (12, 18), (18, 22)]
EPS = 1e-6
MASKED = -1e30
NRING = 4
AHEAD = 2
POOL_LO = (1, 3, 5)

PARAMS = {}
_n = 0
for _name, _w in (
    ("c", 4 * KD), ("norm1", 2 * KD), ("norm2", 2 * KD), ("ada_b", 2 * 48), ("mod_b", 2 * 24),
    ("ffn_w", 2 * 3 * FT), ("ffn_b", 2 * FT), ("qa_g", 3), ("kva_g", 2), ("mq_g", 1), ("mk_g", 1),
    ("gq_g", 1), ("gk_g", 1), ("ml_w", 3 * KD), ("ml_b", KD), ("gate_i", 1), ("gate_f", 1),
    ("out_g", HEADS), ("pre_g", 2 * KD), ("post_g", 2 * KD), ("sink", 2 * HEADS),
    ("sc_w", 2 * 3 * 2), ("sc_b", 2 * 2), ("sel", 2),
):
    PARAMS[_name] = _n
    _n += _w
NPARAM = _n


class Job:

    def __init__(self, kind, src, layer, k, cols, row=0, **more):
        self.kind, self.src, self.layer, self.k, self.cols, self.row = kind, src, layer, k, cols, row
        self.m = sum(c[1] for c in cols)
        self.t0 = more.pop("t0", 0)
        self.more = more
        self.n = None
        self.sq = None


def stream(jobs):
    return ("jobs", jobs)


def ada_jobs(src, layer, blk, a, b):
    return [Job("ada", src, layer, 2, [(c * 4 * P, 4 * P)], row=q * 2 * P, blk=blk, group=c, q=q)
            for c in range(a // 4, b // 4) for q in range(KD // 2)]


def mixed(main, extra, per=1):
    out, extra = [], list(extra)
    for j in main:
        out.append(j)
        out += extra[:per]
        extra = extra[per:]
    return out + extra


def ffn_jobs(layer, t0):
    out = []
    for g, (a, b) in enumerate(GROUPS):
        for i in range(a, b):
            out.append(Job("gate", "ffn_w_up", layer, KD, [(i * P, P)], t0=t0, i=i, g=g, at=i - a))
            out.append(Job("val", "ffn_w_up", layer, KD, [(FF + i * P, P)], t0=t0, i=i, g=g, at=i - a))
        for m in range(KD):
            out.append(Job("addx", "ffn_w_down", layer, b - a, [(m * P, P)], row=a * P, t0=t0, col=m,
                           blk=layer, gate=40, rhs="hid", step=("down", layer, g, m)))
    return out


def plan():
    ph = []
    ph.append(("cvec",))
    ph.append(stream(ada_jobs("ada_w", 0, 0, 0, 16)))
    ph.append(("norm", dict(id="a1", t0=0, g="norm1", gl=0, blk=0, shift=0, scale=8)))
    even = [Job("keep", "att_w_in", 0, KD, [(i * P, P)], dst="CQ", at=i) for i in range(3)]
    even += [Job("keep", "att_w_in", 0, KD, [(384 + i * P, P)], dst="CKV", at=i) for i in range(2)]
    even += [Job("krope", "att_w_in", 0, KD, [(None, 64), (640, 32)])]
    ph.append(stream(even))
    base = 672
    even = [Job("qk", "att_w_in", 0, KD, [(base + j * 64, 64), (base + (j + 4) * 64, 64)], dst="GQ", at=j,
                g="gq_g", norm="BLK64", dim=64, rope="G") for j in range(4)]
    even += [Job("qk", "att_w_in", 0, KD, [(base + 512, P)], dst="GK", at=0, g="gk_g", norm="BLK64", dim=64,
                 rope="G")]
    even += [Job("tokmaj", "att_w_in", 0, KD, [(base + 640, P)], dst="VG", at=0, width=P, rhs="h")]
    ph.append(stream(mixed(even, ada_jobs("ada_w", 0, 0, 16, 24), 2)))
    ph.append(("lownorm",))
    even = [Job("qk", "mla_w_qb", 0, 3, [(h * 96, 96)], dst="MQ", at=h, g="mq_g", norm="ONES", dim=96,
                rope="M", rhs="hid") for h in range(HEADS)]
    even += [Job("kh", "mla_w_kvb", 0, 2, [(h * P, 64), (None, 64)], at=h, rhs="hid", lo=3) for h in range(HEADS)]
    even += [Job("tokmaj", "mla_w_kvb", 0, 2, [(2 * i * P + 64, 64), ((2 * i + 1) * P + 64, 64)], dst="VM",
                 at=i, width=512, rhs="hid", lo=3) for i in range(4)]
    ph.append(stream(mixed(even, ada_jobs("ada_w", 0, 0, 24, 48), 1)))
    ph.append(("attn", "even"))
    ph.append(("turn", dict(id="t_even", tiles=8, q0=0, mul=None)))
    ph.append(stream([Job("addx", "att_w_out", 0, KD, [(m * P, P)], col=m, blk=0, gate=16, rhs="h",
                          step=("attout", m)) for m in range(KD)]))
    ph.append(("norm", dict(id="a2", t0=0, g="norm2", gl=0, blk=0, shift=24, scale=32)))
    ph.append(stream(mixed(ffn_jobs(0, 0), ada_jobs("ada_w", 1, 1, 0, 48))))
    ph.append(("norm", dict(id="b1", t0=0, g="norm1", gl=1, blk=1, shift=0, scale=8)))
    odd = [Job("gates", "ml_w_in", 0, KD, [(3072 + 8 * r, 8), (None, 24), (3072 + 16 + 8 * r, 8), (None, 88)],
               which=r) for r in range(2)]
    odd += [Job("mlqk", "ml_w_in", 0, KD, [(i * P, P)], i=i, t0=CTX if i < 4 else 0) for i in range(8)]
    odd += [Job("tokmaj", "ml_w_in", 0, KD, [(D + i * P, P)], dst="MV", at=i, width=D, rhs="h") for i in range(8)]
    odd += [Job("osig", "ml_w_in", 0, KD, [(2 * D + i * P, P)], i=i, t0=CTX) for i in range(8)]
    ph.append(stream(odd))
    ph.append(("mlstm",))
    ph.append(stream([Job("addx", "ml_w_out", 0, KD, [(m * P, P)], col=m, blk=1, gate=16, rhs="hl", t0=CTX,
                          step=("mlout", m)) for m in range(KD)]))
    ph.append(("norm", dict(id="b2", t0=CTX, g="norm2", gl=1, blk=1, shift=24, scale=32)))
    ph.append(("reload",))
    ph.append(stream(mixed(ffn_jobs(1, CTX), ada_jobs("w_mod_2", 0, 2, 0, 24) + ada_jobs("w_mod_2", 1, 3, 0, 24))))
    for l in range(2):
        t0 = 0 if l == 0 else CTX
        ph.append(("norm", dict(id=f"s{l}", t0=0, g="pre_g", gl=l, blk=2 + l, shift=0, scale=8)))
        s = [Job("qk", "w_in_2", l, KD, [(j * 64, 64), ((j + 4) * 64, 64)], dst="SQT", at=j, scale=0.125, rope="G",
                 t0=t0) for j in range(4)]
        s += [Job("qk", "w_in_2", l, KD, [(512, P)], dst="SK", at=0, scale=1.0, rope="G")]
        s += [Job("tokmaj", "w_in_2", l, KD, [(640, P)], dst="SV", at=0, width=P, rhs="h")]
        s += [Job("silu", "w_in_2", l, KD, [(768 + i * P, P)], dst="GA", at=i, t0=t0) for i in range(4)]
        s += [Job("keep", "w_in_2", l, KD, [(1280 + i * P, P)], dst="UF", at=i, t0=t0) for i in range(2)]
        s += [Job("silu", "w_in_2", l, KD, [(1536 + i * P, P)], dst="SGF", at=i, t0=t0) for i in range(2)]
        s += [Job("keep", "w_in_2", l, KD, [(1792 + i * P, P)], dst="CV", at=i, t0=t0) for i in range(2)]
        s += [Job("cc", "w_in_2", l, KD, [(2304 + i * P, P)], at=i, t0=t0, l=l) for i in range(2)]
        s += [Job("bc", "w_in_2", l, KD, [(2048 + i * P, P)], at=i, t0=t0) for i in range(2)]
        s += [Job("gc", "w_in_2", l, KD, [(2560 + i * P, P)], at=i, t0=t0) for i in range(2)]
        ph.append(stream(s))
        ph.append(("attn", f"win{l}"))
        ph.append(("fourier", l))
        ph.append(("turn", dict(id=f"t_s{l}", tiles=4, q0=t0 // P, mul="GA")))
        ph.append(("merge", l))
        ph.append(stream([Job("yout", "w_out_2", l, KD, [(m * P, P)], col=m, rhs="h", t0=t0) for m in range(KD)]))
        ph.append(("post", l))
    return ph


def staged(js):
    out, mains, group = [], [], None
    for j in js:
        out.append((0, j))
        if group:
            out.append((1, group))
            group = None
        if j.kind == "ada":
            group = j if j.more["q"] == KD // 2 - 1 else None
            continue
        mains.append(j)
        if len(mains) >= 2:
            out.append((1, mains[-2]))
        if len(mains) >= 3:
            out.append((2, mains[-3]))
    if group:
        out.append((1, group))
    if mains:
        out.append((1, mains[-1]))
    out += [(2, j) for j in mains[-2:]]
    late = []
    for stage, j in out:
        late.append((stage, j))
        if stage == 0:
            i = js.index(j)
            late += [(3 + d, js[i - 1 - d]) for d in range(2) if i > d and js[i - 1 - d].sq]
    return late + [(3 + d, js[-1 - e]) for e, d in ((0, 0), (1, 1), (0, 1)) if js[-1 - e].sq]


def numbered():
    ph = plan()
    for a, p in zip(ph, ph[1:]):
        if p[0] == "norm" and a[0] == "jobs":
            last = a[1][3:3 + KD] if p[1]["id"] == "a1" else a[1][-KD:]
            for k, j in enumerate(last):
                j.sq = (p[1], k)
    n = alt = 0
    for p in ph:
        if p[0] == "jobs":
            for j in p[1]:
                j.n = n
                n += 1
                j.alt = alt % 2
                alt += j.kind != "ada"
    return ph, [j for p in ph if p[0] == "jobs" for j in p[1]]


def conv_halves(t0):
    return [(0, LAT)] if t0 else [(0, CTX), (CTX, TOK)]


def segs(t0):
    return [(0, 0, LAT)] if t0 else [(1, 0, CTX), (0, CTX, TOK)]


class Steps:

    def __init__(self):
        self.at, self.known, self.sems = {}, False, {}

    def __call__(self, *key):
        name, value = self.at[key] if self.known else ("dve_done", 0)
        return self.sems[name], value


class Engine:

    def __init__(self, eng, name, steps):
        self.eng, self.name, self.steps = eng, name, steps
        self.count = 0
        self.seen = {}

    def wait_ge(self, sem, value):
        if value > self.seen.get(id(sem), 0):
            self.eng.wait_ge(sem, value)
            self.seen[id(sem)] = value

    def own(self):
        return self.steps.sems[self.name], self.count

    def mark(self, *key):
        self.count += 1
        self.also(*key)
        return self.steps.sems[self.name], 1

    def also(self, *key):
        if key:
            self.steps.at[key] = (self.name, self.count)


def build_program(nc, dram, step):
    phases, jobs = numbered()
    ctx = ExitStack()
    base = 16512
    kb = 1024

    def sb(name, shape, off, dt=F32):
        return nc.alloc_sbuf_tensor_at(name, shape, dt, offset=base + int(off * kb))

    X = sb("X", [P, KD, TOK], 0)
    HH = sb("HH", [P, KD, TOK], 24, F32R)
    HL = sb("HL", [P, KD, TOK], 48, F32R)
    RAW = sb("RAW", [P, NRING, KD * P], 72)
    WL = sb("WL", [P, NRING, KD * P], 72, F32R)
    WH = sb("WH", [P, NRING, KD * P], 88, F32R)
    DH = sb("DH", [P, 6, TOK], 104, F32R)
    DL = sb("DL", [P, 6, TOK], 122, F32R)
    T = [sb(f"T{i}", [P, TOK], 173 + 3 * i)[:, :] for i in range(6)]
    TR = sb("TR", [P, 4, LAT], 191)
    rope = {"G": (TR[:, 0, :], TR[:, 1, :]), "M": (TR[0:96, 2, :], TR[0:96, 3, :])}
    CONST = sb("CONST", [P, 7, P], 199)
    IDENT, ONES, BLK64, ROTG, ROTM, GE, LE = (CONST[:, i, :] for i in range(7))
    PAR = sb("PAR", [P, NPARAM], 202.5)
    MOD = sb("MOD", [P, 288], 202.5 + (NPARAM * 4 + 31) // 32 / 32)
    rest = 202.5 + (NPARAM * 4 + 31) // 32 / 32 + 1.125
    AB = sb("AB", [P, 2, KD], rest)
    STAT = sb("STAT", [P, 64], rest + 0.0625)
    CVF = sb("CVF", [P, 2, KD, 2], rest + 0.3125)
    CV4 = sb("CV4", [P, 2, KD, 4], rest + 0.4375, F32R)
    NE = sb("NE", [P, 4, 64], rest + 0.6875)
    assert base + (rest + 1.6875) * kb <= 229344, rest
    EPSC = STAT[:, 60:61]
    AR = [sb(f"AR{i}", [4, 4 * P], (137, 150)[i])[:, :] for i in range(2)]
    CQ = sb("CQ", [P, 3, TOK], 140)
    CKV = sb("CKV", [P, 2, TOK], 149)
    VM = sb("VM", [P, 6, 512], 140)
    GQ = sb("GQ", [P, 4, TOK], 155)
    GK = sb("GK", [P, 1, TOK], 167)
    VG = sb("VG", [P, 6, P], 170)
    MQ = sb("MQ", [96, HEADS, TOK], 24)
    MK = sb("MK", [96, HEADS, TOK], 48)
    OT = sb("OT", [P, 6, D], 104)
    KR = T[5]
    RT_GQ = sb("RT_GQ", [P, LAT], 104)
    RT_MQ = sb("RT_MQ", [P, LAT], 152)
    LH = sb("LH", [P, KD, LAT], 24, F32R)
    LL = sb("LL", [P, KD, LAT], 48, F32R)
    TX = [sb(f"TX{i}", [P, TOK], o)[:, :] for i, o in enumerate((40, 43, 64, 67))]
    LQ = sb("LQ", [P, 4, LAT], 104)
    LK = sb("LK", [P, 4, TOK], 112)
    MV = sb("MV", [P, 6, D], 124)
    OS = sb("OS", [P, KD, LAT], 148)
    GR = sb("GR", [64, 3, TOK], 164)
    SQT = sb("SQT", [P, 4, TOK], 104)
    SK = sb("SK", [P, 1, TOK], 116)
    SV = sb("SV", [P, 6, P], 119)
    GA = sb("GA", [P, 4, TOK], 122)
    UF = sb("UF", [P, 2, TOK], 134)
    SGF = sb("SGF", [P, 2, TOK], 140)
    CV = sb("CV", [P, 2, TOK], 146)
    Y = sb("Y", [P, 2, TOK], 152)
    OS2 = sb("OS2", [P, 6, 512], 158)
    FV = sb("FV", [P, 6, 512], 24)
    FTT = sb("FTT", [P, 2, TOK], 36)
    DFL = sb("DFL", [P, 2, 4, LAT], 48)
    DFC = sb("DFC", [P, 2, 2, CTX], 64)
    DFW = sb("DFW", [P, 4, P], 68)
    YB = sb("YB", [P, KD, TOK], 104)
    ring_of = dict(CQ=CQ, CKV=CKV, GQ=GQ, GK=GK, VG=VG, MQ=MQ, VM=VM, MV=MV, SQT=SQT, SK=SK, SV=SV, GA=GA,
                   UF=UF, SGF=SGF, CV=CV)

    pairs = [ctx.enter_context(nc.psum_tensor(f"pair{i}", [P, D], F32)) for i in range(3)]
    side = [ctx.enter_context(nc.psum_tensor(f"side{i}", [P, LAT], F32)) for i in range(2)]

    def sem(name):
        return ctx.enter_context(nc.semaphore(name))

    step.sems = {n: sem(n) for n in ("pe_done", "act_done", "dve_done", "pool_done")}
    w_loaded = [sem(f"w_loaded{i}") for i in range(NRING)]
    consts_loaded = sem("consts_loaded")
    ctx_reloaded = sem("ctx_reloaded")
    dft_loaded = sem("dft_loaded")
    stored = sem("stored")

    block = ctx.enter_context(nc.Block())
    offs = []
    o = 0
    for j in jobs:
        offs.append(o)
        o += P * j.k * j.m

    def par(name, i=0, p=P):
        c = PARAMS[name] + i
        return PAR[0:p, c:c + 1]

    def par2(name, p=4):
        return PAR[0:p, PARAMS[name]:PARAMS[name] + 2]

    def squares(j):
        return j.kind == "kh" or (j.kind == "qk" and "norm" in j.more)

    def vrow(j):
        return T[j.alt] if j.layer == 0 and j.src in ("att_w_in", "mla_w_kvb") else T[2 + j.alt]

    def modcol(blk):
        return [0, 96, 192, 240][blk]

    def modv(blk, m, s):
        c = modcol(blk) + 2 * m + s
        return MOD[:, c:c + 1]

    def attn_units(which):
        units = []

        def unit(**kw):
            units.append(kw)

        if which == "even":
            for h in range(HEADS):
                for qt in range(6):
                    L = CTX if qt < 2 else TOK
                    unit(q=MQ[:, h, qt * P:qt * P + P], k=[(0, MK[:, h, 0:L])], L=L, v=[VM[:, i, h * 64:h * 64 + 64] for i in range(L // P)],
                         dst=OT[:, qt, h * 64:h * 64 + 64], masks=[], sink=None)
            for h in range(HEADS):
                b = 64 * (h // 4)
                for qt in range(6):
                    L = CTX if qt < 2 else TOK
                    unit(q=GQ[b:b + 64, h % 4, qt * P:qt * P + P], k=[(0, GK[b:b + 64, 0, 0:L])], L=L,
                         v=[VG[:, i, b:b + 64] for i in range(L // P)],
                         dst=OT[:, qt, 512 + h * 64:512 + h * 64 + 64], masks=[], sink=None)
        else:
            l = int(which[3])
            for h in range(HEADS):
                b = 64 * (h // 4)
                for qt in range(0 if l == 0 else 2, 6):
                    masks = []
                    tiles = [0, 1]
                    if qt >= 2:
                        near = [i for i in (qt - 1, qt, qt + 1) if 2 <= i < 6]
                        for n, i in enumerate(near):
                            if i == qt - 1:
                                masks.append((CTX + n * P, GE))
                            if i == qt + 1:
                                masks.append((CTX + n * P, LE))
                        tiles += near
                    ks = [(0, SK[b:b + 64, 0, 0:CTX])]
                    if qt >= 2:
                        ks.append((CTX, SK[b:b + 64, 0, near[0] * P:near[-1] * P + P]))
                    unit(q=SQT[b:b + 64, h % 4, (qt * P - (0 if l == 0 else CTX)):(qt * P - (0 if l == 0 else CTX)) + P], k=ks, L=len(tiles) * P,
                         v=[SV[:, i, b:b + 64] for i in tiles], dst=OS2[:, qt, h * 64:h * 64 + 64],
                         masks=masks, sink=par("sink", l * HEADS + h))
        return units

    def ln_exp(act, dst, src, dim, key):
        n = dst.shape[0]
        act.wait_ge(*act.own())
        nc.scalar.activation(dst, src, AF.Ln, bias=EPSC[0:n, :], scale=1.0 / dim).then_inc(*act.mark(*(key + ("ln",))))
        act.wait_ge(*act.own())
        nc.scalar.activation(dst, dst, AF.Exp, scale=-0.5).then_inc(*act.mark(*(key)))

    def mA(u):
        return (T[0], T[1]) if u % 2 == 0 else (T[2], T[3])

    def mPT(u):
        return (T[4], T[5])[u % 2]

    def mG(d):
        return TX[d]

    def fkey(l):
        return max(j.n for j in jobs if j.kind == "gc" and j.layer == l)

    def mlstm_pe(pe, mm, take, free, uses):
        for i in range(4):
            take(2)
            pe.wait_ge(*step("nrows"))
            for r in range(2):
                ins = nc.tensor.transpose(pairs[2][:, r * 64:r * 64 + 64], GR[0:64, 1 + r, CTX + i * P:CTX + i * P + P], IDENT[0:64, 0:64])
            ins.then_inc(*pe.mark("ncols", i))
            free[2] = [("ncolread", i)]

        pe.wait_ge(*step("psum_read", max(j.n for j in jobs if j.kind == "osig")))

        def scores(u):
            h, j = u // 4, u % 4
            if j == 0:
                for d in range(2):
                    pr = uses[0] % 2
                    uses[0] += 1
                    take(pr)
                    r = 32 * d + h
                    for c in (0, 512):
                        e = min(TOK, c + 512)
                        ins = mm(pairs[pr][:, c:e], IDENT[0:64, r:r + 1].to_broadcast([64, P]), GR[0:64, 0, c:e], start=True, stop=True)
                    ins.then_inc(*pe.mark("g", h, d))
                    free[pr] = [("gread", h, d)]
            pr = uses[0] % 2
            uses[0] += 1
            take(pr)
            b = 64 * (h % 2)
            for c in (0, 512):
                e = min(TOK, c + 512)
                ins = mm(pairs[pr][:, c:e], LQ[b:b + 64, h // 2, j * P:j * P + P], LK[b:b + 64, h // 2, c:e], start=True, stop=True)
            ins.then_inc(*pe.mark("ms", u))
            free[pr] = [("decayed", u)]

        def turn(u):
            h, j = u // 4, u % 4
            take(2)
            pe.wait_ge(*step("diags", u))
            f, b = mA(u)
            for i in range(6):
                c = i * P if i < 3 else 512 + (i - 3) * P
                parts = []
                if i < 2 or i - 2 <= j:
                    parts.append((f, 0))
                if i < 2 or i - 2 >= j:
                    parts.append((b, 1))
                for n, (a, d) in enumerate(parts):
                    ins = mm(pairs[2][:, c:c + P], a[:, i * P:i * P + P], TX[3][:, (2 * (u % 2) + d) * P:(2 * (u % 2) + d + 1) * P],
                             start=n == 0, stop=n == len(parts) - 1)
            ins.then_inc(*pe.mark("mpt", u))
            free[2] = [("mpta", u), ("mptb", u)]

        def pv(u):
            h, j = u // 4, u % 4
            bank = f"side{h % 2}"
            if j == 0:
                take(bank)
            pe.wait_ge(*step("mpta", u))
            pe.wait_ge(*step("mptb", u))
            for i in range(6):
                ins = mm(side[h % 2][:, j * P:j * P + P], MV[:, i, h * P:h * P + P], mPT(u)[:, i * P:i * P + P], start=i == 0, stop=i == 5)
            ins.then_inc(*pe.mark("mpv", u))
            if j == 3:
                free[bank] = [("hnorm", h)]

        def readout(h):
            take(2)
            pe.wait_ge(*step("hsq", h))
            ins = mm(pairs[2][:, 0:LAT], ONES, TX[2][:, 0:LAT], start=True, stop=True)
            ins.then_inc(*pe.mark("hss", h))
            free[2] = [("hrstd", h, "ln")]

        n = 4 * HEADS
        scores(0)
        scores(1)
        turn(0)
        for u in range(n):
            if u + 2 < n:
                scores(u + 2)
            if u + 1 < n:
                turn(u + 1)
            pv(u)
            if u % 4 == 1 and u > 4:
                readout(u // 4 - 1)
        readout(HEADS - 1)

    def prev_val(j, back):
        i, l = j.more["i"] - back, j.layer
        return (l, i) if i >= 0 else ((l - 1, FT + i) if l else (0, 0))

    def mlstm_act(act, A, uses):
        act.wait_ge(*step("gates_ready"))
        for i in range(4):
            act.wait_ge(*step("ncols", i))
            act.wait_ge(*act.own())
            A(TX[2][:, LAT + i * 128 // 2:LAT + i * 64 + 64], pairs[2][:, 0:64], AF.Copy, scale=1.0).then_inc(*act.mark())
            act.wait_ge(*act.own())
            A(T[i][:, 0:64], pairs[2][:, 64:128], AF.Exp).then_inc(*act.mark("ncolread", i))
            act.wait_ge(*act.own())
            A(NE[:, i, :], T[i][:, 0:64], AF.Copy, scale=1.0).then_inc(*act.mark("ne", i))

        def nM(j, d, h):
            c = LAT + j * 64 + 32 * d + h
            return TX[2][:, c:c + 1]

        pr_of = {}

        def plan_uses(u):
            if u % 4 == 0:
                pr_of[("g", u // 4, 0)] = uses[0] % 2
                pr_of[("g", u // 4, 1)] = (uses[0] + 1) % 2
                uses[0] += 2
            pr_of[u] = uses[0] % 2
            uses[0] += 1

        def gcopy(h):
            for d in range(2):
                act.wait_ge(*step("g", h, d))
                if h >= 1:
                    act.wait_ge(*step("dmask", 4 * h - 1))
                act.wait_ge(*act.own())
                A(mG(d), pairs[pr_of[("g", h, d)]][:, 0:TOK], AF.Copy, scale=1.0).then_inc(*act.mark("gread", h, d))

        def decays(u):
            h, j = u // 4, u % 4
            f, b = mA(u)
            if u >= 2:
                act.wait_ge(*step("mpt", u - 2))
            G0, G1 = mG(0), mG(1)
            dg = CTX + P * j
            act.wait_ge(*act.own())
            A(f[:, 0:dg], G0[:, 0:dg], AF.Exp, bias=nM(j, 0, h)).then_inc(*act.mark())
            act.wait_ge(*act.own())
            A(b[:, 0:CTX], G1[:, 0:CTX], AF.Exp, bias=nM(j, 1, h)).then_inc(*act.mark())
            if j < 3:
                act.wait_ge(*act.own())
                A(b[:, dg + P:TOK], G1[:, dg + P:TOK], AF.Exp, bias=nM(j, 1, h)).then_inc(*act.mark())
            act.wait_ge(*step("dmask", u))
            act.wait_ge(*act.own())
            A(f[:, dg:dg + P], f[:, dg:dg + P], AF.Exp, bias=nM(j, 0, h)).then_inc(*act.mark())
            act.wait_ge(*act.own())
            A(b[:, dg:dg + P], b[:, dg:dg + P], AF.Exp, bias=nM(j, 1, h)).then_inc(*act.mark("decay", u))

        def evict(u):
            act.wait_ge(*step("mpt", u))
            if u >= 2:
                act.wait_ge(*step("mpv", u - 2))
            act.wait_ge(*act.own())
            A(mPT(u)[:, 0:3 * P], pairs[2][:, 0:3 * P], AF.Copy, scale=1.0).then_inc(*act.mark("mpta", u))

        def readout(h, part):
            if part == 0:
                act.wait_ge(*step("mpv", 4 * h + 3))
                if h >= 1:
                    act.wait_ge(*step("hfin", h - 1))
                act.wait_ge(*act.own())
                A(TX[2][:, 0:LAT], side[h % 2][:, :], AF.Square).then_inc(*act.mark("hsq", h))
            elif part == 1:
                act.wait_ge(*step("hss", h))
                ln_exp(act, TX[2][:, 0:LAT], pairs[2][:, 0:LAT], P, ("hrstd", h))
            else:
                act.wait_ge(*step("hmul", h))
                act.wait_ge(*act.own())
                nc.scalar.copy(LH[:, h, :], TX[2][:, 0:LAT]).then_inc(*act.mark("hhi", h))

        n = 4 * HEADS

        def prep(u):
            plan_uses(u)
            if u % 4 == 0:
                gcopy(u // 4)
            decays(u)

        prep(0)
        prep(1)
        evict(0)
        for u in range(n):
            if u + 2 < n:
                prep(u + 2)
            if u + 1 < n:
                evict(u + 1)
            if u % 4 == 0 and u >= 4:
                readout(u // 4 - 1, 0)
            if u % 4 == 1 and u >= 4:
                readout(u // 4 - 1, 1)
            if u % 4 == 2 and u >= 4:
                readout(u // 4 - 1, 2)
        for part in range(3):
            readout(HEADS - 1, part)

    def mlstm_dve(dve, V, uses):
        TT, STT, TS = V.tensor_tensor, V.scalar_tensor_tensor, V.tensor_scalar
        dve.wait_ge(*step("softplus"))
        dve.wait_ge(*step("mlsilu", 7))
        F, S2 = T[0][0:64, :], T[1][0:64, :]
        dve.wait_ge(*dve.own())
        STT(F, GR[:, 1, :], 0.0, T[5][0:64, :], ALU.min, ALU.subtract).then_inc(*dve.mark())
        dve.wait_ge(*dve.own())
        V.memset(T[4][0:64, :], 1.0).then_inc(*dve.mark())
        one = T[4]
        dve.wait_ge(*dve.own())
        V.tensor_tensor_scan(S2[0:32, :], one[0:32, :], F[0:32, :], 0.0, ALU.mult, ALU.add).then_inc(*dve.mark())
        dve.wait_ge(*dve.own())
        V.tensor_tensor_scan(S2[32:64, CTX - 1::-1], one[32:64, 0:CTX], F[32:64, CTX - 1::-1], 0.0, ALU.mult, ALU.add).then_inc(*dve.mark())
        dve.wait_ge(*dve.own())
        V.tensor_tensor_scan(S2[32:64, TOK - 1:CTX - 1:-1], one[32:64, 0:LAT], F[32:64, TOK - 1:CTX - 1:-1], S2[32:64, 0:1], ALU.mult, ALU.add).then_inc(*dve.mark())
        G, M = GR[:, 0, :], T[0][0:64, :]
        dve.wait_ge(*dve.own())
        TT(G, G, S2, ALU.subtract).then_inc(*dve.mark())
        dve.wait_ge(*dve.own())
        V.tensor_tensor_scan(M[0:32, :], G[0:32, :], G[0:32, :], 0.0, ALU.max, ALU.max).then_inc(*dve.mark())
        dve.wait_ge(*dve.own())
        V.tensor_tensor_scan(M[32:64, CTX - 1::-1], G[32:64, CTX - 1::-1], G[32:64, CTX - 1::-1], 0.0, ALU.max, ALU.max).then_inc(*dve.mark())
        dve.wait_ge(*dve.own())
        V.tensor_tensor_scan(M[32:64, TOK - 1:CTX - 1:-1], G[32:64, TOK - 1:CTX - 1:-1], G[32:64, TOK - 1:CTX - 1:-1], M[32:64, 0:1], ALU.max, ALU.max).then_inc(*dve.mark())
        dve.wait_ge(*dve.own())
        TS(GR[:, 1, :], M, -1.0, None, ALU.mult).then_inc(*dve.mark())
        dve.wait_ge(*dve.own())
        TT(GR[:, 2, :], GR[:, 1, :], S2, ALU.subtract).then_inc(*dve.mark("nrows"))
        dve.also("gates_ready")
        dve.wait_ge(*step("ne", 3))

        pr_of = {}
        cnt = [uses[0]]

        def plan_uses(u):
            if u % 4 == 0:
                cnt[0] += 2
            pr_of[u] = cnt[0] % 2
            cnt[0] += 1

        def masks(u):
            h, j = u // 4, u % 4
            plan_uses(u)
            f, b = mA(u)
            dg = CTX + P * j
            if j == 0:
                dve.wait_ge(*step("gread", h, 1))
            if u >= 2:
                dve.wait_ge(*step("mpt", u - 2))
            dve.wait_ge(*dve.own())
            TT(f[:, dg:dg + P], mG(0)[:, dg:dg + P], LE, ALU.add).then_inc(*dve.mark())
            dve.wait_ge(*dve.own())
            TT(b[:, dg:dg + P], mG(1)[:, dg:dg + P], GE, ALU.add).then_inc(*dve.mark("dmask", u))

        def weigh(u):
            h, j = u // 4, u % 4
            f, b = mA(u)
            dg = CTX + P * j
            st = 16 * (u % 3)
            S = pairs[pr_of[u]]
            c = [STAT[:, st + i:st + i + 1] for i in range(6)]
            dve.wait_ge(*step("ms", u))
            dve.wait_ge(*step("decay", u))
            ttr = V.tensor_tensor_reduce
            kw = dict(scale=0.125, scalar=0.0, op0=ALU.mult, op1=ALU.add)
            dve.wait_ge(*dve.own())
            ttr(out=f[:, 0:dg + P], in0=f[:, 0:dg + P], in1=S[:, 0:dg + P], accum_out=c[0], **kw).then_inc(*dve.mark())
            dve.wait_ge(*dve.own())
            ttr(out=b[:, 0:CTX], in0=b[:, 0:CTX], in1=S[:, 0:CTX], accum_out=c[1], **kw).then_inc(*dve.mark())
            dve.wait_ge(*dve.own())
            ttr(out=b[:, dg:TOK], in0=b[:, dg:TOK], in1=S[:, dg:TOK], accum_out=c[2], **kw).then_inc(*dve.mark("decayed", u))
            dve.wait_ge(*dve.own())
            TT(c[1], c[1], c[2], ALU.add).then_inc(*dve.mark())
            both, size = STAT[:, st:st + 2], STAT[:, st + 3:st + 5]
            dve.wait_ge(*dve.own())
            STT(size, both, -1.0, both, ALU.mult, ALU.max).then_inc(*dve.mark())
            dve.wait_ge(*dve.own())
            TT(size, size, NE[:, j, h:h + 33:32], ALU.max).then_inc(*dve.mark())
            dve.wait_ge(*dve.own())
            V.reciprocal(STAT[:, st + 5:st + 7], STAT[:, st + 3:st + 5]).then_inc(*dve.mark())
            if u >= 2:
                dve.wait_ge(*step("mpt", u - 2))
            for d in range(2):
                q = (2 * (u % 2) + d) * P
                dve.wait_ge(*dve.own())
                TS(TX[3][:, q:q + P], IDENT, STAT[:, st + 5 + d:st + 6 + d], None, ALU.mult).then_inc(*dve.mark(*(("diags", u) if d else ("diag0", u))))

        def evict(u):
            dve.wait_ge(*step("mpt", u))
            if u >= 2:
                dve.wait_ge(*step("mpv", u - 2))
            dve.wait_ge(*dve.own())
            V.tensor_copy(mPT(u)[:, 3 * P:6 * P], pairs[2][:, 512:512 + 3 * P]).then_inc(*dve.mark("mptb", u))

        def readout(h):
            dve.wait_ge(*step("hrstd", h))
            R = TX[2][:, 0:LAT]
            dve.wait_ge(*dve.own())
            STT(R, side[h % 2][:, :], par("out_g", h), R, ALU.mult, ALU.mult).then_inc(*dve.mark("hnorm", h))
            dve.wait_ge(*dve.own())
            TT(R, R, OS[:, h, :], ALU.mult).then_inc(*dve.mark("hmul", h))
            dve.wait_ge(*step("hhi", h))
            dve.wait_ge(*dve.own())
            TT(LL[:, h, :], R, LH[:, h, :].bitcast(F32), ALU.subtract).then_inc(*dve.mark("hmix", h))
            dve.also("hfin", h)

        n = 4 * HEADS
        masks(0)
        weigh(0)
        masks(1)
        weigh(1)
        evict(0)
        for u in range(n):
            if u + 2 < n:
                masks(u + 2)
                weigh(u + 2)
            if u + 1 < n:
                evict(u + 1)
            if u % 4 == 2 and u >= 4:
                readout(u // 4 - 1)
        readout(HEADS - 1)
        uses[0] = cnt[0]

    @block.tensor
    def _(eng):
        pe = Engine(eng, "pe_done", step)
        free = {}
        uses = [0]
        mm = nc.tensor.matmul
        state = {"hready": [], "first": True}

        def take(bank):
            for key in free.pop(bank, []):
                pe.wait_ge(*step(*key))

        def job(j):
            s = j.n % NRING
            wh, wl = ([t[:, s, k * j.m:(k + 1) * j.m] for k in range(j.k)] for t in (WH, WL))
            if j.kind == "ada":
                q, b = j.more["q"], 0 if j.src == "ada_w" else 1
                if j.n == 0:
                    pe.wait_ge(*step("cvec"))
                if q == 0:
                    take("side1")
                pe.wait_ge(*step("lo", j.n))
                for k in range(j.k):
                    c = CV4[:, b, q * j.k + k, :]
                    mm(side[1][0:4, :], c, wh[k], start=q == 0 and k == 0, stop=False)
                    ins = mm(side[1][0:4, :], c, wl[k], start=False, stop=q == KD // 2 - 1 and k == j.k - 1)
                free["side1"] = [("arow", j.more["blk"], j.more["group"])]
                ins.then_inc(*pe.mark("mm", j.n))
                return
            pr = uses[0] % 2
            uses[0] += 1
            take(pr)
            pe.wait_ge(*step("lo", j.n))
            out = pairs[pr]
            src = j.more.get("rhs", "h")
            lo = j.more.get("lo", 0)
            if src == "hid":
                rh, rl = DH, DL
            elif src == "hl":
                rh, rl = LH, LL
            else:
                rh, rl = HH, HL
            off = 0 if src == "hl" or (src == "hid" and j.t0) else j.t0
            n = TOK - j.t0
            for c in range(0, n, 512):
                e = min(n, c + 512)
                for k in range(j.k):
                    pe_wait_rhs(j, src, k + lo)
                    a, b = rh[:, lo + k, off + c:off + e], rl[:, lo + k, off + c:off + e]
                    mm(out[0:j.m, c:e], wh[k], a, start=k == 0, stop=False)
                    mm(out[0:j.m, c:e], wh[k], b, start=False, stop=False)
                    ins = mm(out[0:j.m, c:e], wl[k], a, start=False, stop=k == j.k - 1)
            ins.then_inc(*pe.mark("mm", j.n))
            free[pr] = [("psum_read", j.n)]
            j.pair = pr

        def pe_wait_rhs(j, src, k):
            if src == "hid" and j.kind == "addx":
                pe.wait_ge(*step("hid", j.layer, j.more["step"][2], k))
            elif src == "hid":
                pe.wait_ge(*step("low", k))
            else:
                for key in state["hready"]:
                    pe.wait_ge(*step(*key, k))

        def sums(sq, ones, n, rows, key, wait):
            take(2)
            pe.wait_ge(*step(*wait))
            for c in range(0, n, 512):
                e = min(n, c + 512)
                ins = mm(pairs[2][0:rows, c:e], ones[0:rows, 0:rows], sq[0:rows, c:e], start=True, stop=True)
            ins.then_inc(*pe.mark(*key))

        for p in phases:
            if p[0] == "cvec":
                pe.wait_ge(consts_loaded, 16 * 4)
            elif p[0] == "jobs":
                js = p[1]
                for stage, j in staged(js):
                    if stage == 0:
                        job(j)
                    if stage == 1:
                        if j.kind == "ada":
                            key = j.more["blk"], j.more["group"]
                            take(2)
                            pe.wait_ge(*step("arow", *key))
                            for f in range(4):
                                ins = mm(pairs[2][:, 2 * f:2 * f + 2], AR[key[0] > 0][:, f * P:f * P + P], par2("sel"), start=True, stop=True)
                            ins.then_inc(*pe.mark("acol", *key))
                            free[2] = [("mod",) + (key[0], 4 * key[1])]
                        if j.kind == "qk" and "norm" in j.more:
                            sums(T[j.alt], BLK64 if j.more["norm"] == "BLK64" else ONES, TOK, j.m, ("ss", j.n), ("sq", j.n))
                            free[2] = [("rstd", j.n, "ln")]
                        if j.kind == "tokmaj":
                            take(2)
                            pe.wait_ge(*step("vrow", j.n))
                            for i in range(6):
                                ins = nc.tensor.transpose(pairs[2][:, i * P:i * P + P], vrow(j)[:, i * P:i * P + P], IDENT)
                            ins.then_inc(*pe.mark("vturn", j.n))
                            free[2] = [("vdone", j.n)]
                        if j.kind == "kh":
                            sums(T[j.alt], ONES, TOK, 96, ("ss", j.n), ("sq", j.n))
                            free[2] = [("rstd", j.n, "ln")]
                    if stage == 2:
                        if (j.kind == "qk") or j.kind == "krope":
                            take("side0")
                            pe.wait_ge(*step("scaled", j.n))
                            b = KR[0:96, :] if j.kind == "krope" else ring_of[j.more["dst"]][0:j.m, j.more["at"], :]
                            lat0 = CTX - j.t0
                            rot = ROTM if j.kind == "krope" or j.more["rope"] == "M" else ROTG
                            ins = mm(side[0][0:j.m, :], rot[0:j.m, 0:j.m], b[:, lat0:lat0 + LAT], start=True, stop=True)
                            ins.then_inc(*pe.mark("rot", j.n))
                            free["side0"] = [("rotread", j.n)]
            elif p[0] == "norm":
                q = p[1]
                n = TOK - q["t0"]
                sums(T[2], ONES, n, P, ("nss", q["id"]), ("nacc", q["id"]))
                free[2] = [("nrstd", q["id"], "ln")]
                state["hready"] = [("hlo", q["id"])]
            elif p[0] == "lownorm":
                for name, sqs in (("cq", 3), ("ckv", 2)):
                    take(2)
                    for k in range(sqs):
                        pe.wait_ge(*step("lsq", name, k))
                        for c in (0, 512):
                            e = min(TOK, c + 512)
                            ins = mm(pairs[2][:, c:e], ONES, T[k][:, c:e], start=k == 0, stop=k == sqs - 1, skip_group_check=True)
                    ins.then_inc(*pe.mark("lss", name))
                    free[2] = [("lrstd", name, "ln")]
            elif p[0] == "attn":
                units = attn_units(p[1])
                w = p[1]
                pe.wait_ge(*step("ready", w))
                pe.wait_ge(*step("ready_act", w))

                def scores(u):
                    x = units[u]
                    pr = uses[0] % 2
                    uses[0] += 1
                    take(pr)
                    out = pairs[pr]
                    pieces = []
                    for c0, k in x["k"]:
                        n = k.shape[-1]
                        edges = {512 - c0} | {e - c0 for m in x["masks"] for e in (m[0], m[0] + P)}
                        cuts = sorted(c for c in edges if 0 < c < n)
                        for a, b in zip([0] + cuts, cuts + [n]):
                            pieces.append((c0 + a, c0 + b, k[:, a:b]))
                    for a, b, k in pieces:
                        ms = [m for m in x["masks"] if a <= m[0] < b]
                        ins = mm(out[:, a:b], x["q"], k, start=True, stop=not ms)
                        for c, mask in ms:
                            ins = mm(out[:, c:c + P], IDENT, mask, start=False, stop=True)
                    ins.then_inc(*pe.mark("s", w, u))
                    free[pr] = [("exp", w, u)]

                def turn(u):
                    x = units[u]
                    nt = x["L"] // P
                    half = nt - nt // 2
                    take(2)
                    pe.wait_ge(*step("exp", w, u))
                    for i in range(nt):
                        c = i * P if i < half else 512 + (i - half) * P
                        ins = nc.tensor.transpose(pairs[2][:, c:c + P], T[u % 2][:, i * P:i * P + P], IDENT)
                    ins.then_inc(*pe.mark("pt", w, u))
                    free[2] = [("pta", w, u), ("ptb", w, u)]

                def pv(u):
                    x = units[u]
                    take(f"side{u % 2}")
                    pe.wait_ge(*step("pta", w, u))
                    pe.wait_ge(*step("ptb", w, u))
                    nt = x["L"] // P
                    for i in range(nt):
                        ins = mm(side[u % 2][:, 0:64], T[2 + u % 2][:, i * P:i * P + P], x["v"][i], start=i == 0, stop=i == nt - 1)
                    ins.then_inc(*pe.mark("pv", w, u))
                    free[f"side{u % 2}"] = [("o", w, u)]

                scores(0)
                scores(1)
                turn(0)
                for u in range(len(units)):
                    if u + 2 < len(units):
                        scores(u + 2)
                    if u + 1 < len(units):
                        turn(u + 1)
                    pv(u)
            elif p[0] == "turn":
                q = p[1]
                src = OT if q["tiles"] == 8 else OS2
                pe.wait_ge(*step("attn_end", q["id"]))
                for qt in range(q["q0"], 6):
                    for half in range(q["tiles"] // 4):
                        pr = uses[0] % 2
                        uses[0] += 1
                        take(pr)
                        for i in range(4):
                            f = half * 4 + i
                            ins = nc.tensor.transpose(pairs[pr][:, i * P:i * P + P], src[:, qt, f * P:f * P + P], IDENT)
                        ins.then_inc(*pe.mark("ot", q["id"], qt, half))
                        free[pr] = [("otread", q["id"], qt, half)]
                state["hready"] = [("hturn", q["id"])] if q["tiles"] == 8 else []
            elif p[0] == "mlstm":
                mlstm_pe(pe, mm, take, free, uses)
                state["hready"] = [("hmix",)]
            elif p[0] == "fourier":
                l = p[1]
                t0 = 0 if l == 0 else CTX
                tiles = list(range(t0 // P, 6))
                pe.wait_ge(dft_loaded, 16 * 3 * (l + 1))
                for i in tiles:
                    pr = uses[0] % 2
                    uses[0] += 1
                    take(pr)
                    pe.wait_ge(*step("psum_read", fkey(l)))
                    for cs in range(2):
                        for f in range(2):
                            c = (cs * 2 + f) * P
                            ins = mm(pairs[pr][:, c:c + P], UF[:, f, i * P - t0:i * P - t0 + P], DFW[:, cs, :], start=True, stop=True)
                    ins.then_inc(*pe.mark("fv", l, i))
                    free[pr] = [("fvread", l, i)]
                for f in range(2):
                    pr = uses[0] % 2
                    uses[0] += 1
                    take(pr)
                    for i in tiles:
                        pe.wait_ge(*step("fvread", l, i))
                    out = pairs[pr]
                    seq = [(cs, i) for cs in range(2) for i in range(4)]
                    for x, (cs, i) in enumerate(seq):
                        ins = mm(out[:, 0:LAT], FV[:, 2 + i, (cs * 2 + f) * P:(cs * 2 + f + 1) * P], DFL[:, cs, i, :], start=x == 0, stop=x == 7)
                    if l == 0:
                        seq = [(cs, i) for cs in range(2) for i in range(2)]
                        for x, (cs, i) in enumerate(seq):
                            ins = mm(out[:, LAT:TOK], FV[:, i, (cs * 2 + f) * P:(cs * 2 + f + 1) * P], DFC[:, cs, i, :], start=x == 0, stop=x == 3)
                    ins.then_inc(*pe.mark("fdft", l, f))
                    free[pr] = [("fdftread", l, f)]
                for f in range(2):
                    pr = uses[0] % 2
                    uses[0] += 1
                    take(pr)
                    pe.wait_ge(*step("fdftread", l, f))
                    n = TOK - t0
                    for c in range(0, n, 512):
                        e = min(n, c + 512)
                        ins = mm(pairs[pr][:, c:e], DFW[:, 2 + f, :], FTT[:, f, c:e], start=True, stop=True)
                    ins.then_inc(*pe.mark("fw", l, f))
                    free[pr] = [("fwread", l, f)]
            elif p[0] == "merge":
                state["hready"] = [("merged", p[1])]
            elif p[0] == "post":
                l = p[1]
                n = TOK if l == 0 else LAT
                sums(T[2], ONES, n, P, ("pss", l), ("pacc", l))
                free[2] = [("prstd", l, "ln")]

    @block.scalar
    def _(eng):
        act = Engine(eng, "act_done", step)
        A = nc.scalar.activation
        nsplit = [0]

        def split():
            if nsplit[0] == len(jobs):
                return
            j = jobs[nsplit[0]]
            nsplit[0] += 1
            act.wait_ge(w_loaded[j.n % NRING], 16 * (j.n // NRING + 1))
            c = j.k * j.m
            act.wait_ge(*act.own())
            nc.scalar.copy(WH[:, j.n % NRING, 0:c], RAW[:, j.n % NRING, 0:c]).then_inc(*act.mark("hi", j.n))

        def epilogue(j, pr):
            n = TOK - j.t0
            ps = pairs[pr][:, 0:n]
            m = j.more
            if j.kind == "ada":
                key = m["blk"], m["group"]
                if m["q"] == KD // 2 - 1:
                    act.wait_ge(*step("mm", j.n))
                    if key[1] or key[0]:
                        act.wait_ge(*step("acol", *((key[0], key[1] - 1) if key[1] else (key[0] - 1, (12, 12, 6)[key[0] - 1] - 1))))
                    act.wait_ge(*act.own())
                    A(AR[key[0] > 0], side[1][0:4, :], AF.Copy, scale=1.0).then_inc(*act.mark("arow", *key))
            elif j.kind == "keep":
                act.wait_ge(*step("mm", j.n))
                act.wait_ge(*act.own())
                A(ring_of[m["dst"]][:, m["at"], 0:n], ps, AF.Identity).then_inc(*act.mark("psum_read", j.n))
            elif j.kind == "silu":
                act.wait_ge(*step("mm", j.n))
                act.wait_ge(*act.own())
                A(ring_of[m["dst"]][:, m["at"], 0:n], ps, AF.Silu).then_inc(*act.mark("psum_read", j.n))
            elif j.kind == "krope":
                act.wait_ge(*step("mm", j.n))
                act.wait_ge(*act.own())
                A(T[4][0:96, :], pairs[pr][0:96, 0:TOK], AF.Square).then_inc(*act.mark("krsq"))
                act.wait_ge(*act.own())
                A(KR[0:96, :], pairs[pr][0:96, 0:TOK], AF.Copy, scale=1.0).then_inc(*act.mark("psum_read", j.n))
            elif j.kind == "tokmaj":
                act.wait_ge(*step("mm", j.n))
                act.wait_ge(*step("sqfree", j.n))
                act.wait_ge(*act.own())
                A(vrow(j), pairs[pr][:, 0:TOK], AF.Copy, scale=1.0).then_inc(*act.mark("vrow", j.n))
                act.also("psum_read", j.n)
            elif j.kind == "qk":
                act.wait_ge(*step("mm", j.n))
                if "norm" in m:
                    if j.n >= 2:
                        act.wait_ge(*step("sqfree", j.n))
                    act.wait_ge(*act.own())
                    A(T[j.alt][0:j.m, :], pairs[pr][0:j.m, 0:TOK], AF.Square).then_inc(*act.mark("sq", j.n))
                else:
                    act.wait_ge(*act.own())
                    A(ring_of[m["dst"]][:, m["at"], 0:n], ps, AF.Copy, scale=m["scale"]).then_inc(*act.mark("psum_read", j.n))
                    act.also("scaled", j.n)
            elif j.kind == "kh":
                act.wait_ge(*step("mm", j.n))
                act.wait_ge(*step("krsqcopy", j.n))
                act.wait_ge(*act.own())
                A(T[j.alt][0:64, :], pairs[pr][0:64, 0:TOK], AF.Square).then_inc(*act.mark("sq", j.n))
            elif j.kind == "gate":
                act.wait_ge(*step("mm", j.n))
                i = m["i"]
                if (j.layer, i) != (0, 0):
                    act.wait_ge(*step("val", *prev_val(j, 2)))
                act.wait_ge(*act.own())
                A(T[i % 2][:, 0:n], ps, AF.Identity, scale=par("ffn_w", (j.layer * 3 + 1) * FT + i), bias=par("ffn_b", j.layer * FT + i)).then_inc(*act.mark("cmid", j.n))
            elif j.kind == "val":
                i = m["i"]
                act.wait_ge(*step("conv", j.layer, i))
                act.wait_ge(*act.own())
                A(T[i % 2][:, 0:n], T[i % 2][:, 0:n], AF.Silu).then_inc(*act.mark("silu", j.n))
            elif j.kind == "mlqk":
                i = m["i"]
                act.wait_ge(*step("mm", j.n))
                if i >= 2:
                    act.wait_ge(*step("mlsilu", i - 2))
                act.wait_ge(*act.own())
                A(T[i % 2][:, 0:n], ps, AF.Identity, scale=par("ml_w", KD + i), bias=par("ml_b", i)).then_inc(*act.mark("cmid", j.n))
                if i >= 1:
                    mlsilu(i - 1)
            elif j.kind == "osig":
                i = m["i"]
                act.wait_ge(*step("mm", j.n))
                act.wait_ge(*act.own())
                A(OS[:, i, :], ps, AF.Sigmoid).then_inc(*act.mark("psum_read", j.n))
            elif j.kind == "gates":
                act.wait_ge(*step("mm", j.n))
                r = m["which"]
                act.wait_ge(*step("grzero"))
                rows = pairs[pr][0:64, 0:TOK]
                if r == 0:
                    act.wait_ge(*act.own())
                    A(GR[:, 0, :], rows, AF.Identity, bias=PAR[0:64, PARAMS["gate_i"]:PARAMS["gate_i"] + 1]).then_inc(*act.mark("psum_read", j.n))
                else:
                    act.wait_ge(*act.own())
                    A(GR[:, 1, :], rows, AF.Identity, bias=PAR[0:64, PARAMS["gate_f"]:PARAMS["gate_f"] + 1]).then_inc(*act.mark("psum_read", j.n))
                    act.wait_ge(*act.own())
                    A(T[5][0:64, :], GR[:, 1, :], AF.Abs).then_inc(*act.mark())
                    act.wait_ge(*act.own())
                    A(T[5][0:64, :], T[5][0:64, :], AF.Exp, scale=-1.0).then_inc(*act.mark())
                    act.wait_ge(*act.own())
                    A(T[5][0:64, :], T[5][0:64, :], AF.Ln, bias=1.0).then_inc(*act.mark("softplus"))
            elif j.kind == "gc":
                act.wait_ge(*step("mm", j.n))
                act.wait_ge(*step("ymul", j.layer, m["at"]))
                act.wait_ge(*act.own())
                A(T[m["at"]][:, 0:n], ps, AF.Silu).then_inc(*act.mark("psum_read", j.n))
            elif j.kind == "yout":
                act.wait_ge(*step("mm", j.n))
                i = m["col"]
                act.wait_ge(*act.own())
                A(YB[:, i, 0:n], ps, AF.Copy, scale=1.0).then_inc(*act.mark())
                if i >= 2:
                    act.wait_ge(*step("pacc", j.layer, i - 2))
                act.wait_ge(*act.own())
                A(T[i % 2][:, 0:n], ps, AF.Square).then_inc(*act.mark("psum_read", j.n))

        def square(q, k):
            n = TOK - q["t0"]
            if k >= 3:
                act.wait_ge(*step("nacc", q["id"], k - 2))
            act.wait_ge(*act.own())
            A(T[k % 2 if k else 2][:, 0:n], X[:, k, q["t0"]:TOK], AF.Square).then_inc(*act.mark("nsq", q["id"], k))

        def mlsilu(i):
            act.wait_ge(*step("mlconv", i))
            if i < 4:
                act.wait_ge(*act.own())
                A(LQ[:, i, :], T[i % 2][:, 0:LAT], AF.Silu).then_inc(*act.mark("mlsilu", i))
            else:
                act.wait_ge(*act.own())
                A(LK[:, i - 4, :], T[i % 2], AF.Silu).then_inc(*act.mark("mlsilu", i))

        act.wait_ge(consts_loaded, 16 * 4)
        uses = [0]
        for pi, p in enumerate(phases):
            act.also("act_end", pi)
            if p[0] in ("norm", "lownorm", "attn", "mlstm", "post"):
                act.wait_ge(*step("dve_end", pi))
            if p[0] == "cvec":
                act.wait_ge(*act.own())
                A(CVF[:].rearrange("p b k s -> p (b k s)"), PAR[:, 0:4 * KD], AF.Silu).then_inc(*act.mark("csilu"))
                act.wait_ge(*act.own())
                nc.scalar.copy(CV4[:, :, :, 0:2], CVF[:]).then_inc(*act.mark("chi"))
                act.wait_ge(*step("eps"))
                for _ in range(AHEAD):
                    split()
            elif p[0] == "jobs":
                js = p[1]
                for stage, j in staged(js):
                    if stage == 0:
                        split()
                        epilogue(j, uses[0] % 2)
                        uses[0] += j.kind != "ada"
                    if stage == 3:
                        q, k = j.sq
                        if j.kind == "addx":
                            act.wait_ge(*step("xcol", j.n))
                            if j.src == "ffn_w_down" and k == 0:
                                act.wait_ge(*step("hidr", j.layer, FT - 1))
                        if q["id"] == "s0" and k == 0:
                            act.wait_ge(ctx_reloaded, 16)
                        square(q, k)
                    if stage == 1:
                        if (j.kind == "qk" and "norm" in j.more) or j.kind == "kh":
                            act.wait_ge(*step("ss", j.n))
                            act.wait_ge(*step("rfree", j.n))
                            rows = 96 if j.kind == "kh" else j.m
                            ln_exp(act, T[2 + j.alt][0:rows, :], pairs[2][0:rows, 0:TOK], j.more.get("dim", 96), ("rstd", j.n))
                        if j.kind == "mlqk" and j.more["i"] == 7:
                            mlsilu(7)
                nxt = phases[pi + 1]
                if nxt[0] == "attn":
                    act.also("ready_act", nxt[1])
            elif p[0] == "norm":
                q = p[1]
                t0, n = q["t0"], TOK - q["t0"]
                act.wait_ge(*step("xready", q["id"]))
                act.wait_ge(*step("nss", q["id"]))
                ln_exp(act, T[3][:, 0:n], pairs[2][:, 0:n], D, ("nrstd", q["id"]))
                for k in range(KD):
                    t = (T[0], T[1], T[4], T[5])[k % 4]
                    act.wait_ge(*step("nmul", q["id"], k))
                    for s, a, b in segs(t0):
                        dst = t[:, a:b] if k in POOL_LO else HH[:, k, t0 + a:t0 + b]
                        act.wait_ge(*act.own())
                        A(dst, t[:, a:b], AF.Identity, bias=modv(q["blk"], q["shift"] + k, s)).then_inc(*act.mark())
                    if k in POOL_LO:
                        act.wait_ge(*act.own())
                        nc.scalar.copy(HH[:, k, t0:TOK], t[:, 0:n]).then_inc(*act.mark())
                    act.also("nhi", q["id"], k)
            elif p[0] == "lownorm":
                for name, src, g in (("cq", CQ, "qa_g"), ("ckv", CKV, "kva_g")):
                    nk = src.shape[1]
                    for k in range(nk):
                        if name == "ckv":
                            act.wait_ge(*step("lss", "cq"))
                        act.wait_ge(*act.own())
                        A(T[k], src[:, k, :], AF.Square).then_inc(*act.mark("lsq", name, k))
                    act.wait_ge(*step("lss", name))
                    act.wait_ge(*step("lowr", name))
                    ln_exp(act, T[3], pairs[2][:, 0:TOK], nk * P, ("lrstd", name))
                act.wait_ge(*step("low", 4))
            elif p[0] == "attn":
                w = p[1]
                units = attn_units(w)
                if w != "even":
                    l = int(w[3])
                    act.wait_ge(*step("mm", fkey(l)))
                    for dst, name in ((DFL, "dft_lat"), (DFC, "dft_ctx")):
                        act.eng.dma_start(dst[:], dram[name]).then_inc(dft_loaded, 16)
                    act.eng.dma_start(DFW[:], dram["dft_w"][l]).then_inc(dft_loaded, 16)

                def exps(u):
                    x = units[u]
                    act.wait_ge(*step("nmax", w, u))
                    if u >= 2:
                        act.wait_ge(*step("pt", w, u - 2))
                    st = 8 * (u % 4)
                    if x["sink"] is not None:
                        act.wait_ge(*act.own())
                        A(STAT[:, st + 3:st + 4], x["sink"], AF.Exp, bias=STAT[:, st + 1:st + 2]).then_inc(*act.mark())
                    pr = uses[0] % 2
                    uses[0] += 1
                    act.wait_ge(*act.own())
                    A(T[u % 2][:, 0:x["L"]], pairs[pr][:, 0:x["L"]], AF.Exp, bias=STAT[:, st + 1:st + 2], accum_out=STAT[:, st + 2:st + 3]).then_inc(*act.mark("exp", w, u))

                def evict(u):
                    x = units[u]
                    nt = x["L"] // P
                    half = nt - nt // 2
                    act.wait_ge(*step("pt", w, u))
                    if u >= 2:
                        act.wait_ge(*step("pv", w, u - 2))
                    act.wait_ge(*act.own())
                    A(T[2 + u % 2][:, 0:half * P], pairs[2][:, 0:half * P], AF.Copy, scale=1.0).then_inc(*act.mark("pta", w, u))

                act.wait_ge(*step("attn_free", w))
                exps(0)
                evict(0)
                exps(1)
                for u in range(len(units)):
                    if u + 1 < len(units):
                        evict(u + 1)
                    if u + 2 < len(units):
                        exps(u + 2)
                uses[0] += 0
            elif p[0] == "turn":
                q = p[1]
                for qt in range(q["q0"], 6):
                    for half in range(q["tiles"] // 4):
                        pr = uses[0] % 2
                        uses[0] += 1
                        if q["mul"] is None:
                            act.wait_ge(*step("ot", q["id"], qt, half))
                            act.wait_ge(*act.own())
                            nc.scalar.copy(HH[:, half * 4:half * 4 + 4, qt * P:qt * P + P], pairs[pr][:, 0:512].rearrange("p (f t) -> p f t", t=P)).then_inc(*act.mark("othi", q["id"], qt, half))
                        else:
                            act.wait_ge(*step("otmul", q["id"], qt, half))
                            act.wait_ge(*act.own())
                            nc.scalar.copy(HH[:, 0:4, qt * P:qt * P + P], T[qt % 2][:, 0:512].rearrange("p (f t) -> p f t", t=P)).then_inc(*act.mark("othi", q["id"], qt, half))
            elif p[0] == "mlstm":
                mlstm_act(act, A, uses)
            elif p[0] == "fourier":
                l = p[1]
                t0 = 0 if l == 0 else CTX
                tiles = list(range(t0 // P, 6))
                for i in tiles:
                    pr = uses[0] % 2
                    uses[0] += 1
                    act.wait_ge(*step("fv", l, i))
                    act.wait_ge(*act.own())
                    A(FV[:, i, :], pairs[pr][:, 0:512], AF.Copy, scale=1.0).then_inc(*act.mark("fvread", l, i))
                for f in range(2):
                    pr = uses[0] % 2
                    uses[0] += 1
                    act.wait_ge(*step("fdft", l, f))
                    lat0 = CTX - t0
                    act.wait_ge(*act.own())
                    A(FTT[:, f, lat0:lat0 + LAT], pairs[pr][:, 0:LAT], AF.Copy, scale=1.0).then_inc(*act.mark("fdftread", l, f, 0))
                    if l == 0:
                        act.wait_ge(*act.own())
                        A(FTT[:, f, 0:CTX], pairs[pr][:, LAT:TOK], AF.Copy, scale=1.0).then_inc(*act.mark())
                    act.also("fdftread", l, f)
                uses[0] += 2
            elif p[0] == "merge":
                l = p[1]
                t0 = 0 if l == 0 else CTX
                n = TOK - t0
                for i in range(2):
                    act.wait_ge(*step("fwread", l, i))
                    act.wait_ge(*act.own())
                    nc.scalar.copy(HH[:, 4 + i, t0:TOK], UF[:, i, 0:n]).then_inc(*act.mark("mhi", l, i))
                for i in range(2):
                    act.wait_ge(*step("ydone", l, i))
                    act.wait_ge(*act.own())
                    nc.scalar.copy(HH[:, 6 + i, t0:TOK], Y[:, i, 0:n]).then_inc(*act.mark("mhi", l, 2 + i))
            elif p[0] == "post":
                l = p[1]
                n = TOK if l == 0 else LAT
                act.wait_ge(*step("pss", l))
                ln_exp(act, T[3][:, 0:n], pairs[2][:, 0:n], D, ("prstd", l))
                if l == 0:
                    for k in range(KD):
                        act.wait_ge(*step("xfin", 0, k))
                        square(phases[pi + 1][1], k)
            elif p[0] == "reload":
                act.wait_ge(*step("xctx_free"))
                act.wait_ge(*step("nmul", "b1", KD - 1))
                act.eng.dma_start(X[:, :, 0:CTX], dram["ctx2"]).then_inc(ctx_reloaded, 16)

    @block.vector
    def _(eng):
        dve = Engine(eng, "dve_done", step)
        V = nc.vector
        TT, STT, TS = V.tensor_tensor, V.scalar_tensor_tensor, V.tensor_scalar
        nsplit = [0]
        uses = [0]

        def split():
            if nsplit[0] == len(jobs):
                return
            j = jobs[nsplit[0]]
            nsplit[0] += 1
            dve.wait_ge(*step("hi", j.n))
            c = j.k * j.m
            dve.wait_ge(*dve.own())
            TT(WL[:, j.n % NRING, 0:c], RAW[:, j.n % NRING, 0:c], WH[:, j.n % NRING, 0:c].bitcast(F32), ALU.subtract).then_inc(*dve.mark("lo", j.n))

        def taps(dst, ps, t0, w0, w2, key):
            for a, b in conv_halves(t0):
                dve.wait_ge(*dve.own())
                STT(dst[:, a + 1:b], ps[:, a:b - 1], w0, dst[:, a + 1:b], ALU.mult, ALU.add).then_inc(*dve.mark())
                dve.wait_ge(*dve.own())
                STT(dst[:, a:b - 1], ps[:, a + 1:b], w2, dst[:, a:b - 1], ALU.mult, ALU.add).then_inc(*dve.mark())
            dve.also(*key)

        def epilogue(j, pr):
            n = TOK - j.t0
            ps = pairs[pr][:, 0:n]
            m = j.more
            if j.kind == "krope":
                dve.wait_ge(*step("psum_read", j.n))
                dve.wait_ge(*dve.own())
                TS(KR[0:96, :], KR[0:96, :], par("mk_g", p=96), None, ALU.mult).then_inc(*dve.mark("scaled", j.n))
            elif j.kind == "kh":
                dve.wait_ge(*step("ssfree", j.n))
                dve.wait_ge(*dve.own())
                V.tensor_copy(T[j.alt][64:96, :], T[4][64:96, :]).then_inc(*dve.mark("krsqcopy", j.n))
            elif j.kind == "gate":
                i = m["i"]
                dve.wait_ge(*step("cmid", j.n))
                taps(T[i % 2], ps, j.t0, par("ffn_w", j.layer * 3 * FT + i), par("ffn_w", (j.layer * 3 + 2) * FT + i), ("conv", j.layer, i))
                dve.also("psum_read", j.n)
            elif j.kind == "val":
                i = m["i"]
                dve.wait_ge(*step("silu", j.n))
                dve.wait_ge(*step("mm", j.n))
                if (j.layer, i) not in ((0, 0), (0, 1)):
                    dve.wait_ge(*step("hidr", *prev_val(j, 2)))
                dve.wait_ge(*dve.own())
                TT(T[2 + i % 2][:, 0:n], T[i % 2][:, 0:n], ps, ALU.mult).then_inc(*dve.mark("val", j.layer, i))
                dve.also("psum_read", j.n)
            elif j.kind == "addx":
                dve.wait_ge(*step("mm", j.n))
                for s, a, b in segs(j.t0):
                    x = X[:, m["col"], j.t0 + a:j.t0 + b]
                    dve.wait_ge(*dve.own())
                    STT(x, pairs[pr][:, a:b], modv(m["blk"], m["gate"] + m["col"], s), x, ALU.mult, ALU.add).then_inc(*dve.mark())
                dve.also("psum_read", j.n)
            elif j.kind == "mlqk":
                i = m["i"]
                dve.wait_ge(*step("cmid", j.n))
                taps(T[i % 2], ps, j.t0, par("ml_w", i), par("ml_w", 2 * KD + i), ("mlconv", i))
                dve.also("psum_read", j.n)
            elif j.kind == "cc":
                i, l = m["at"], m["l"]
                dve.wait_ge(*step("mm", j.n))
                dve.wait_ge(*step("psum_read", j.n - 2))
                dve.wait_ge(*dve.own())
                TT(CV[:, i, 0:n], CV[:, i, 0:n], ps, ALU.mult).then_inc(*dve.mark("psum_read", j.n))
                w = [par("sc_w", (l * 3 + t) * 2 + i) for t in range(3)]
                dve.wait_ge(*dve.own())
                TS(Y[:, i, 0:n], CV[:, i, 0:n], w[1], par("sc_b", l * 2 + i), ALU.mult, ALU.add).then_inc(*dve.mark())
                taps(Y[:, i, :], CV[:, i, :], j.t0, w[0], w[2], ("yconv", l, i))
            elif j.kind == "bc":
                dve.wait_ge(*step("mm", j.n))
                dve.wait_ge(*dve.own())
                TT(Y[:, m["at"], 0:n], Y[:, m["at"], 0:n], ps, ALU.mult).then_inc(*dve.mark("psum_read", j.n))
                dve.also("ymul", j.layer, m["at"])
            elif j.kind == "gc":
                dve.wait_ge(*step("psum_read", j.n))
                dve.wait_ge(*dve.own())
                TT(Y[:, m["at"], 0:n], Y[:, m["at"], 0:n], T[m["at"]][:, 0:n], ALU.mult).then_inc(*dve.mark("ydone", j.layer, m["at"]))
            elif j.kind == "yout":
                i = m["col"]
                dve.wait_ge(*step("psum_read", j.n))
                if i == 0:
                    dve.wait_ge(*dve.own())
                    V.tensor_copy(T[2][:, 0:n], T[0][:, 0:n]).then_inc(*dve.mark("pacc", j.layer, 0))
                else:
                    dve.wait_ge(*dve.own())
                    TT(T[2][:, 0:n], T[2][:, 0:n], T[i % 2][:, 0:n], ALU.add).then_inc(*dve.mark("pacc", j.layer, i))
                if i == KD - 1:
                    dve.also("pacc", j.layer)

        def accumulate(q, k):
            n = TOK - q["t0"]
            dve.wait_ge(*step("nsq", q["id"], k))
            if k:
                dve.wait_ge(*dve.own())
                TT(T[2][:, 0:n], T[2][:, 0:n], T[k % 2][:, 0:n], ALU.add).then_inc(*dve.mark("nacc", q["id"], k))
            if k == KD - 1:
                dve.also("nacc", q["id"])

        def scale_stage(j):
            m = j.more
            if j.kind == "ada":
                blk, g = m["blk"], m["group"]
                c = modcol(blk) + 8 * g
                b = PARAMS["ada_b"] + blk * 48 if blk < 2 else PARAMS["mod_b"] + (blk - 2) * 24
                dve.wait_ge(*step("acol", blk, g))
                for s in range(2):
                    dve.wait_ge(*dve.own())
                    TT(MOD[:, c + s:c + 8:2], pairs[2][:, s:8:2], PAR[:, b + 4 * g:b + 4 * g + 4], ALU.add).then_inc(*dve.mark())
                for i in range(4):
                    dve.also("mod", blk, 4 * g + i)
                return
            if j.kind == "tokmaj":
                dve.wait_ge(*step("vturn", j.n))
                dve.wait_ge(*dve.own())
                V.tensor_copy(ring_of[m["dst"]][:, :, m["at"] * P:m["at"] * P + P], pairs[2][:, 0:TOK].rearrange("p (t n) -> p t n", n=P)).then_inc(*dve.mark("vdone", j.n))
                return
            pr = j.pair_dve
            if j.kind == "qk" and "norm" in m:
                dve.wait_ge(*step("rstd", j.n))
                R = T[2 + j.alt]
                g = par(m["g"], p=j.m)
                dve.wait_ge(*dve.own())
                STT(ring_of[m["dst"]][0:j.m, m["at"], :], pairs[pr][0:j.m, 0:TOK], g, R[0:j.m, :], ALU.mult, ALU.mult).then_inc(*dve.mark("scaled", j.n))
                dve.also("psum_read", j.n)
            elif j.kind == "kh":
                dve.wait_ge(*step("rstd", j.n))
                R = T[2 + j.alt]
                dve.wait_ge(*dve.own())
                STT(MK[0:64, m["at"], :], pairs[pr][0:64, 0:TOK], par("mk_g", p=64), R[0:64, :], ALU.mult, ALU.mult).then_inc(*dve.mark("psum_read", j.n))
                dve.wait_ge(*dve.own())
                TT(MK[64:96, m["at"], :], KR[64:96, :], R[64:96, :], ALU.mult).then_inc(*dve.mark("kready", j.n))

        def rope_stage(j):
            if j.kind not in ("qk", "krope"):
                return
            b = KR[0:96, :] if j.kind == "krope" else ring_of[j.more["dst"]][0:j.m, j.more["at"], :]
            cos, sin = rope["M" if j.kind == "krope" else j.more["rope"]]
            rows = 96 if j.kind == "krope" else j.m
            lat0 = CTX - j.t0
            x = b[0:rows, lat0:lat0 + LAT]
            dve.wait_ge(*step("rot", j.n))
            dve.wait_ge(*dve.own())
            TT(x, x, cos[0:rows, :], ALU.mult).then_inc(*dve.mark())
            t = (RT_MQ if j.more.get("dst") == "MQ" else T[4][:, 0:LAT] if j.src == "w_in_2" else RT_GQ)[0:rows, :]
            dve.wait_ge(*dve.own())
            TT(t, side[0][0:rows, :], sin[0:rows, :], ALU.mult).then_inc(*dve.mark("rotread", j.n))
            dve.wait_ge(*dve.own())
            TT(x, x, t, ALU.add).then_inc(*dve.mark("roped", j.n))

        dve.wait_ge(consts_loaded, 16 * 4)
        for pi, p in enumerate(phases):
            dve.also("dve_end", pi)
            if p[0] in ("norm", "lownorm", "attn", "mlstm", "post"):
                dve.wait_ge(*step("act_end", pi))
            if p[0] == "cvec":
                dve.wait_ge(*dve.own())
                V.memset(EPSC, EPS).then_inc(*dve.mark("eps"))
                dve.wait_ge(*step("chi"))
                dve.wait_ge(*dve.own())
                TT(CV4[:, :, :, 2:4], CVF[:], CV4[:, :, :, 0:2].bitcast(F32), ALU.subtract).then_inc(*dve.mark("cvec"))
                for _ in range(AHEAD):
                    split()
                for name, dim in (("mq_g", 96), ("gq_g", 64)):
                    dve.wait_ge(*dve.own())
                    TS(par(name), par(name), float(dim ** -0.5), None, ALU.mult).then_inc(*dve.mark())
                dve.also("xready", "a1")
            elif p[0] == "jobs":
                js = p[1]
                for stage, j in staged(js):
                    if stage == 0:
                        i = js.index(j)
                        split()
                        j.pair_dve = uses[0] % 2
                        if squares(j) or j.kind == "tokmaj":
                            side_jobs = [x for x in js[:i] if x.alt == j.alt and (squares(x) or x.kind == "tokmaj")]
                            last = side_jobs[-1] if side_jobs else None
                            step.at[("sqfree", j.n)] = step.at.get(("ss" if squares(last) else "vturn", last.n), ("dve_done", 0)) if last else ("dve_done", 0)
                            step.at[("ssfree", j.n)] = step.at[("sqfree", j.n)]
                            side_jobs = [x for x in side_jobs if squares(x)]
                            last = side_jobs[-1] if side_jobs else None
                            step.at[("rfree", j.n)] = step.at.get(("kready" if last.kind == "kh" else "scaled", last.n), ("dve_done", 0)) if last else ("dve_done", 0)
                        epilogue(j, uses[0] % 2)
                        uses[0] += j.kind != "ada"
                        if j.kind == "addx":
                            dve.also("xcol", j.n)
                    if stage == 1:
                        scale_stage(j)
                    if stage == 2:
                        rope_stage(j)
                    if stage == 4:
                        accumulate(*j.sq)
                nxt = phases[pi + 1] if pi + 1 < len(phases) else None
                if nxt and nxt[0] == "norm":
                    dve.also("xready", nxt[1]["id"])
                if nxt and nxt[0] == "attn":
                    dve.also("attn_free", nxt[1])
                    dve.also("ready", nxt[1])
            elif p[0] == "norm":
                q = p[1]
                t0, n = q["t0"], TOK - q["t0"]
                if q["id"] == "s0":
                    dve.wait_ge(ctx_reloaded, 16)
                dve.wait_ge(*step("mod", q["blk"], q["scale"] + KD - 1))
                g = PAR[:, PARAMS[q["g"]] + q["gl"] * KD:PARAMS[q["g"]] + (q["gl"] + 1) * KD]
                for s in range(2):
                    c = modcol(q["blk"]) + 2 * q["scale"] + s
                    dve.wait_ge(*dve.own())
                    STT(AB[:, s, :], MOD[:, c:c + 2 * KD - 1:2], 1.0, g, ALU.add, ALU.mult).then_inc(*dve.mark())
                dve.wait_ge(*step("nrstd", q["id"]))

                def lo(k):
                    if k in POOL_LO:
                        return
                    t = (T[0], T[1], T[4], T[5])[k % 4]
                    dve.wait_ge(*step("nhi", q["id"], k))
                    for s, a, b in segs(t0):
                        dve.wait_ge(*dve.own())
                        STT(HL[:, k, t0 + a:t0 + b], t[:, a:b], modv(q["blk"], q["shift"] + k, s), HH[:, k, t0 + a:t0 + b].bitcast(F32), ALU.add, ALU.subtract).then_inc(*dve.mark("hlo", q["id"], k))

                for k in range(KD):
                    t = (T[0], T[1], T[4], T[5])[k % 4]
                    if k - 4 in POOL_LO:
                        dve.wait_ge(*step("hlo", q["id"], k - 4))
                    for s, a, b in segs(t0):
                        dve.wait_ge(*dve.own())
                        STT(t[:, a:b], X[:, k, t0 + a:t0 + b], AB[:, s, k:k + 1], T[3][:, a:b], ALU.mult, ALU.mult).then_inc(*dve.mark("nmul", q["id"], k))
                    if k >= 2:
                        lo(k - 2)
                lo(KD - 2)
                lo(KD - 1)
            elif p[0] == "lownorm":
                r = 0
                for name, src, g, at in (("cq", CQ, "qa_g", 0), ("ckv", CKV, "kva_g", 3)):
                    dve.also("lowr", name)
                    dve.wait_ge(*step("lrstd", name))
                    for k in range(src.shape[1]):
                        dve.wait_ge(*dve.own())
                        STT(src[:, k, :], src[:, k, :], par(g, k), T[3], ALU.mult, ALU.mult).then_inc(*dve.mark())
                        dve.wait_ge(*dve.own())
                        V.tensor_copy(DH[:, at + k, :], src[:, k, :]).then_inc(*dve.mark())
                        dve.wait_ge(*dve.own())
                        TT(DL[:, at + k, :], src[:, k, :], DH[:, at + k, :].bitcast(F32), ALU.subtract).then_inc(*dve.mark("low", at + k))
            elif p[0] == "attn":
                w = p[1]
                units = attn_units(w)
                u0 = uses[0]

                def negmax(u):
                    x = units[u]
                    st = 8 * (u % 4)
                    dve.wait_ge(*step("s", w, u))
                    pr = (u0 + u) % 2
                    dve.wait_ge(*dve.own())
                    V.tensor_reduce(STAT[:, st:st + 1], pairs[pr][:, 0:x["L"]], AX, ALU.max).then_inc(*dve.mark())
                    if x["sink"] is None:
                        dve.wait_ge(*dve.own())
                        TS(STAT[:, st + 1:st + 2], STAT[:, st:st + 1], -1.0, None, ALU.mult).then_inc(*dve.mark("nmax", w, u))
                    else:
                        dve.wait_ge(*dve.own())
                        TS(STAT[:, st + 1:st + 2], STAT[:, st:st + 1], x["sink"], -1.0, ALU.max, ALU.mult).then_inc(*dve.mark("nmax", w, u))

                def evict(u):
                    x = units[u]
                    nt = x["L"] // P
                    half = nt - nt // 2
                    dve.wait_ge(*step("pt", w, u))
                    if u >= 2:
                        dve.wait_ge(*step("pv", w, u - 2))
                    dve.wait_ge(*dve.own())
                    V.tensor_copy(T[2 + u % 2][:, half * P:nt * P], pairs[2][:, 512:512 + (nt - half) * P]).then_inc(*dve.mark("ptb", w, u))

                def out(u):
                    x = units[u]
                    st = 8 * (u % 4)
                    if x["sink"] is not None:
                        dve.wait_ge(*dve.own())
                        TT(STAT[:, st + 2:st + 3], STAT[:, st + 2:st + 3], STAT[:, st + 3:st + 4], ALU.add).then_inc(*dve.mark())
                    dve.wait_ge(*dve.own())
                    V.reciprocal(STAT[:, st + 4:st + 5], STAT[:, st + 2:st + 3]).then_inc(*dve.mark())
                    dve.wait_ge(*step("pv", w, u))
                    dve.wait_ge(*dve.own())
                    TS(x["dst"], side[u % 2][:, 0:64], STAT[:, st + 4:st + 5], None, ALU.mult).then_inc(*dve.mark("o", w, u))

                negmax(0)
                negmax(1)
                evict(0)
                for u in range(len(units)):
                    if u + 2 < len(units):
                        negmax(u + 2)
                    if u + 1 < len(units):
                        evict(u + 1)
                    out(u)
                uses[0] += len(units)
                tid = {"even": "t_even", "win0": "t_s0", "win1": "t_s1"}[w]
                dve.also("attn_end", tid)
            elif p[0] == "turn":
                q = p[1]
                t0 = q["q0"] * P
                for qt in range(q["q0"], 6):
                    for half in range(q["tiles"] // 4):
                        pr = uses[0] % 2
                        uses[0] += 1
                        cols = slice(half * 4, half * 4 + 4)
                        hi = HH[:, cols, qt * P:qt * P + P].bitcast(F32)
                        lo = HL[:, cols, qt * P:qt * P + P]
                        src = pairs[pr][:, 0:512].rearrange("p (f t) -> p f t", t=P)
                        if q["mul"] is None:
                            dve.wait_ge(*step("othi", q["id"], qt, half))
                            dve.wait_ge(*dve.own())
                            TT(lo, src, hi, ALU.subtract).then_inc(*dve.mark("otread", q["id"], qt, half))
                        else:
                            dve.wait_ge(*step("ot", q["id"], qt, half))
                            t = T[qt % 2][:, 0:512].rearrange("p (f t) -> p f t", t=P)
                            dve.wait_ge(*dve.own())
                            TT(t, src, GA[:, :, qt * P - t0:qt * P - t0 + P], ALU.mult).then_inc(*dve.mark("otread", q["id"], qt, half))
                            dve.also("otmul", q["id"], qt, half)
                            dve.wait_ge(*step("othi", q["id"], qt, half))
                            dve.wait_ge(*dve.own())
                            TT(lo, t, hi, ALU.subtract).then_inc(*dve.mark())
                for k in range(8):
                    dve.also("hturn", q["id"], k)
            elif p[0] == "mlstm":
                mlstm_dve(dve, V, uses)
            elif p[0] == "fourier":
                l = p[1]
                t0 = 0 if l == 0 else CTX
                n = TOK - t0
                uses[0] += (6 if l == 0 else 4) + 2
                for f in range(2):
                    pr = uses[0] % 2
                    uses[0] += 1
                    dve.wait_ge(*step("fw", l, f))
                    dve.wait_ge(*dve.own())
                    TT(UF[:, f, 0:n], pairs[pr][:, 0:n], SGF[:, f, 0:n], ALU.mult).then_inc(*dve.mark("fwread", l, f))
            elif p[0] == "merge":
                l = p[1]
                t0 = 0 if l == 0 else CTX
                n = TOK - t0
                for i, src in enumerate((UF[:, 0, :], UF[:, 1, :], Y[:, 0, :], Y[:, 1, :])):
                    dve.wait_ge(*step("mhi", l, i))
                    dve.wait_ge(*dve.own())
                    TT(HL[:, 4 + i, t0:TOK], src[:, 0:n], HH[:, 4 + i, t0:TOK].bitcast(F32), ALU.subtract).then_inc(*dve.mark())
                for k in range(8):
                    dve.also("merged", l, k)
            elif p[0] == "post":
                l = p[1]
                t0 = 0 if l == 0 else CTX
                n = TOK - t0
                g = PAR[:, PARAMS["post_g"] + l * KD:PARAMS["post_g"] + (l + 1) * KD]
                for s in range(2):
                    c = modcol(2 + l) + 2 * 16 + s
                    dve.wait_ge(*dve.own())
                    TT(AB[:, s, :], MOD[:, c:c + 2 * KD - 1:2], g, ALU.mult).then_inc(*dve.mark())
                dve.wait_ge(*step("prstd", l))
                for k in range(KD):
                    for s, a, b in segs(t0):
                        dve.wait_ge(*dve.own())
                        STT(YB[:, k, a:b], YB[:, k, a:b], AB[:, s, k:k + 1], T[3][:, a:b], ALU.mult, ALU.mult).then_inc(*dve.mark())
                    dve.wait_ge(*dve.own())
                    TT(X[:, k, t0:TOK], X[:, k, t0:TOK], YB[:, k, 0:n], ALU.add).then_inc(*dve.mark("xfin", l, k))
                    if l == 0 and k >= 1:
                        accumulate(phases[pi + 1][1], k - 1)
                if l == 0:
                    accumulate(phases[pi + 1][1], KD - 1)
                    dve.also("xready", "s1")
            if p[0] == "norm" and p[1]["id"] == "b1":
                dve.also("xctx_free")
            if p[0] == "norm" and p[1]["id"] == "b1":
                dve.wait_ge(*dve.own())
                V.memset(GR[:], 0.0).then_inc(*dve.mark("grzero"))

    @block.gpsimd
    def _(eng):
        pool = Engine(eng, "pool_done", step)
        for p in phases:
            if p[0] == "norm":
                q = p[1]
                t0 = q["t0"]
                for k in POOL_LO:
                    t = (T[0], T[1], T[4], T[5])[k % 4]
                    pool.wait_ge(*step("nhi", q["id"], k))
                    pool.wait_ge(*pool.own())
                    nc.gpsimd.tensor_tensor(HL[:, k, t0:TOK], t[:, 0:TOK - t0], HH[:, k, t0:TOK].bitcast(F32), ALU.subtract).then_inc(*pool.mark("hlo", q["id"], k))
            elif p[0] == "jobs":
                for j in p[1]:
                    if j.kind == "val":
                        i, n, at = j.more["i"], TOK - j.t0, j.more["at"]
                        pool.wait_ge(*step("val", j.layer, i))
                        pool.wait_ge(*pool.own())
                        nc.gpsimd.tensor_copy(DH[:, at, 0:n], T[2 + i % 2][:, 0:n]).then_inc(*pool.mark())
                        pool.wait_ge(*pool.own())
                        nc.gpsimd.tensor_tensor(DL[:, at, 0:n], T[2 + i % 2][:, 0:n], DH[:, at, 0:n].bitcast(F32), ALU.subtract).then_inc(*pool.mark("hidr", j.layer, i))
                        pool.also("hid", j.layer, j.more["g"], at)

    @block.sync
    def _(eng):
        sp = Engine(eng, "sp", step)
        eng.dma_start(PAR[:], dram["params"]).then_inc(consts_loaded, 16)
        eng.dma_start(CONST[:], dram["consts"]).then_inc(consts_loaded, 16)
        for j in jobs:
            if j.n >= NRING:
                sp.wait_ge(*step("mm", j.n - NRING))
            c = j.k * j.m
            src = dram["w"][offs[j.n]:offs[j.n] + P * c].rearrange("(p c) -> p c", p=P)
            eng.dma_start(RAW[:, j.n % NRING, 0:c], src).then_inc(w_loaded[j.n % NRING], 16)
            if j.n == 1:
                eng.dma_start(TR[:], dram["rope"]).then_inc(consts_loaded, 16)
                eng.dma_start(X[:], dram["x"]).then_inc(consts_loaded, 16)
        for k in range(KD):
            sp.wait_ge(*step("xfin", 1, k))
            eng.dma_start(dram["out"][k * P:(k + 1) * P, :], X[:, k, CTX:TOK]).then_inc(stored, 16)
        eng.wait_ge(stored, 16 * KD)

    ctx.close()
    step.known = True


def rope_rows(dim, n_freq):
    inv = np.float32(10000.0) ** (-np.arange(n_freq, dtype=np.float32) / np.float32(n_freq))
    t = np.arange(LAT)
    row, col = (t // 64).astype(np.float32), (t % 64).astype(np.float32)
    a = np.concatenate([row[None] * inv[:, None]] * 2 + [col[None] * inv[:, None]] * 2, 0)
    return np.cos(a).astype(np.float32), np.sin(a).astype(np.float32)


def rotation(n, at, block):
    r = np.zeros((P, P), np.float32)
    for s in range(n):
        for half in range(2):
            o = at + s * 4 * block + half * 2 * block
            for i in range(block):
                r[o + block + i, o + i] = -1.0
                r[o + i, o + block + i] = 1.0
    return r


def shape_constants():
    c = np.zeros((P, 7, P), np.float32)
    q, k = np.arange(P)[:, None], np.arange(P)[None]
    c[:, 0] = np.eye(P)
    c[:, 1] = 1.0
    c[:, 2] = (q // 64 == k // 64)
    c[:, 3] = rotation(2, 0, 16)
    c[:, 4] = rotation(1, 64, 8)
    c[:, 5] = np.where(k >= q, 0.0, MASKED)
    c[:, 6] = np.where(k <= q, 0.0, MASKED)
    rope = np.zeros((P, 4, LAT), np.float32)
    rope[0:64, 0], rope[0:64, 1] = rope_rows(64, 16)
    rope[64:128, 0:2] = rope[0:64, 0:2]
    rope[0:64, 2] = 1.0
    rope[64:96, 2], rope[64:96, 3] = rope_rows(32, 8)
    dft = {}
    for name, n in (("dft_lat", LAT), ("dft_ctx", CTX)):
        a = 2 * np.pi * ((np.arange(n)[:, None] * np.arange(n)[None]) % n) / n
        t = np.stack([np.cos(a), -np.sin(a)]) / np.sqrt(n * 64.0)
        dft[name] = t.reshape(2, n // P, P, n).transpose(2, 0, 1, 3).astype(np.float32).copy()
    a = 2 * np.pi * ((np.arange(64)[:, None] * np.arange(64)[None]) % 64) / 64
    chan = np.zeros((P, 2, P), np.float32)
    for s in range(2):
        z = slice(64 * s, 64 * s + 64)
        chan[z, 0, z], chan[z, 1, z] = np.cos(a), np.sin(a)
    return c, rope, dft, chan


def columns(a, p=P):
    a = np.asarray(a)
    return a.reshape(-1, p).T


def lay_out(x):
    consts, rope, dft, chan = shape_constants()
    par = np.zeros((P, NPARAM), np.float32)

    def put(name, a, i=0):
        a = np.asarray(a)
        par[0:a.shape[0], PARAMS[name] + i:PARAMS[name] + i + a.shape[1]] = a

    cv = np.zeros((P, 2, KD, 2), np.float32)
    for b, (c, cc) in enumerate((("c", "c_ctx"), ("c_2", "c_ctx_2"))):
        cv[:, b, :, 0] = columns(x[c])
        cv[:, b, :, 1] = columns(x[cc])
    put("c", cv.reshape(P, -1))
    for name, src in (("norm1", "norm1_g"), ("norm2", "norm2_g"), ("ada_b", "ada_b"), ("mod_b", "b_mod_2"),
                      ("ffn_w", "ffn_conv_w"), ("ffn_b", "ffn_conv_b"), ("qa_g", "mla_qa_g"), ("kva_g", "mla_kva_g"),
                      ("ml_w", "ml_conv_w"), ("ml_b", "ml_conv_b"), ("out_g", "ml_out_g"), ("pre_g", "g_pre_2"),
                      ("post_g", "g_post_2"), ("sc_w", "conv_w_2"), ("sc_b", "conv_b_2")):
        put(name, columns(x[src]))
    put("mq_g", columns(x["mla_q_g"], 96))
    put("mk_g", columns(x["mla_k_g"], 96))
    for name in ("gq_g", "gk_g"):
        g = columns(x["gqa_q_g" if name == "gq_g" else "gqa_k_g"], 64)
        put(name, np.concatenate([g, g], 0))
    gate = np.asarray(x["ml_gate_b"]).reshape(4, HEADS)
    for name, (f, b) in (("gate_i", (0, 2)), ("gate_f", (1, 3))):
        c = np.zeros((64, 1), np.float32)
        c[0:8, 0], c[32:40, 0] = gate[f], gate[b]
        put(name, c)
    put("sel", np.tile(np.eye(2, dtype=np.float32), (2, 1)))
    put("sink", np.broadcast_to(np.asarray(x["sink_2"]).reshape(1, -1), (P, 2 * HEADS)))
    jobs = numbered()[1]
    parts = []
    for j in jobs:
        a = np.asarray(x[j.src])[j.layer][j.row:j.row + j.k * P]
        t = np.zeros((P, j.k, j.m), np.float32)
        o = 0
        for c, n in j.cols:
            if c is not None:
                t[:, :, o:o + n] = a[:, c:c + n].reshape(j.k, P, n).transpose(1, 0, 2)
            o += n
        parts.append(t.reshape(-1))
    w = np.concatenate(parts)
    dw = np.zeros((2, P, 4, P), np.float32)
    wf = np.asarray(x["w_fourier_2"])
    for l in range(2):
        dw[l, :, 0:2] = chan
        for g in range(4):
            z = slice(64 * (g % 2), 64 * (g % 2) + 64)
            dw[l, z, 2 + g // 2, z] = wf[l, g]

    def tokens(a):
        return np.asarray(a)[0].T.reshape(KD, P, -1).transpose(1, 0, 2)

    both = np.concatenate([tokens(x["ctx"]), tokens(x["x"])], 2)
    return dict(w=w, params=par, consts=consts, rope=rope, x=np.ascontiguousarray(both),
                ctx2=np.ascontiguousarray(tokens(x["ctx_2"])), dft_lat=dft["dft_lat"], dft_ctx=dft["dft_ctx"], dft_w=dw)


def tensors(nc, arrays):
    dram = {n: nc.dram_tensor(f"in_{n}", a.shape, F32, kind="ExternalInput").ap() for n, a in arrays.items()}
    dram["out"] = nc.dram_tensor("out_x", (D, LAT), F32, kind="ExternalOutput").ap()
    return dram


def kernel(**inputs):
    import concourse.bacc as bacc
    from concourse.bass_utils import run_bass_kernel_spmd

    arrays = lay_out(inputs)
    step = Steps()
    for _ in range(2):
        nc = bacc.Bacc("TRN2", target_bir_lowering=False, num_devices=1)
        build_program(nc, tensors(nc, arrays), step)
    r = run_bass_kernel_spmd(nc, [{f"in_{n}": a for n, a in arrays.items()}], core_ids=[0])
    return np.ascontiguousarray(r.results[0]["out_x"].T)[None]
```
